# Optimizing a Trainium2 kernel written in Bass

```python
import jax, jax.numpy as jnp
from jax import lax
import numpy as np

D_MODEL = 1024
BATCH = 1
SEQ = 1024
DEPTH = 1

N_Q_HEADS = 8
N_KV_HEADS = 2
HEAD_DIM = 64
Q_GROUP = N_Q_HEADS // N_KV_HEADS
ATTN_WIDTH = N_Q_HEADS * HEAD_DIM
KV_WIDTH = N_KV_HEADS * HEAD_DIM
WINDOW = 128
BLOCK = 128
POOL_WINDOWS = (2, 4, 8, 16)
POOL_GROUPS = len(POOL_WINDOWS)
POOL_WIDTH = D_MODEL // 2
POOL_GROUP_DIM = POOL_WIDTH // POOL_GROUPS
IN_WIDTH = ATTN_WIDTH + 2 * KV_WIDTH + POOL_WIDTH
N_BRANCHES = 2
PEER_HEADS = 8
N_KEYS = 128
N_EXPERTS = N_KEYS * N_KEYS
PEER_HALF = 128
PEER_QUERY_DIM = 2 * PEER_HALF
PEER_TOPK = 16
PEER_CHUNK = 128
EPS = 1e-6
NEG_INF = -1e30

kernel_name = "hybrid_swa_pool_peer_encoder"

def _alibi_slopes():
    s = np.array([2.0 ** (-8.0 * (h + 1) / N_Q_HEADS) for h in range(N_Q_HEADS)], dtype=np.float32)
    return jnp.asarray(s).reshape(N_KV_HEADS, Q_GROUP)

def _rmsnorm(x, g):
    xf = x.astype(jnp.float32)
    y = xf * lax.rsqrt(jnp.mean(xf * xf, axis=-1, keepdims=True) + EPS)
    return (y * g.astype(jnp.float32)).astype(x.dtype)

def _windowed_gqa(q, k, v, sink_logits):
    B, S, _ = q.shape
    nb = S // BLOCK
    qb = q.reshape(B, nb, BLOCK, N_KV_HEADS, Q_GROUP, HEAD_DIM)

    def band(t):
        t = t.reshape(B, S, N_KV_HEADS, HEAD_DIM)
        tp = jnp.pad(t, ((0, 0), (BLOCK, BLOCK), (0, 0), (0, 0)))
        tp = tp.reshape(B, nb + 2, BLOCK, N_KV_HEADS, HEAD_DIM)
        return jnp.concatenate([tp[:, :-2], tp[:, 1:-1], tp[:, 2:]], axis=2)

    kb, vb = band(k), band(v)
    logits = jnp.einsum('bnqkgd,bnckd->bnkgqc', qb, kb).astype(jnp.float32) * (HEAD_DIM ** -0.5)
    qpos = jnp.arange(BLOCK)
    cpos = jnp.arange(3 * BLOCK)
    rel = qpos[:, None] + BLOCK - cpos[None, :]
    dist = jnp.abs(rel)
    s_abs = jnp.arange(nb)[:, None] * BLOCK - BLOCK + cpos[None, :]
    valid = (dist <= WINDOW)[None] & ((s_abs >= 0) & (s_abs < S))[:, None, :]
    logits = logits - _alibi_slopes()[:, :, None, None] * dist.astype(jnp.float32)
    logits = jnp.where(valid[None, :, None, None], logits, NEG_INF)
    sink = jnp.broadcast_to(sink_logits.astype(jnp.float32).reshape(N_KV_HEADS, Q_GROUP, 1, 1),
                            logits.shape[:-1] + (1,))
    probs = jax.nn.softmax(jnp.concatenate([logits, sink], axis=-1), axis=-1)[..., :-1]
    out = jnp.einsum('bnkgqc,bnckd->bnqkgd', probs.astype(v.dtype), vb)
    return out.reshape(B, S, ATTN_WIDTH)

def _pool_mixer(u, pool_w, pool_scale):
    B, S, _ = u.shape
    ug = u.reshape(B, S, POOL_GROUPS, POOL_GROUP_DIM)
    csum = jnp.concatenate([jnp.zeros((B, 1, POOL_GROUPS, POOL_GROUP_DIM), jnp.float32),
                            jnp.cumsum(ug.astype(jnp.float32), axis=1)], axis=1)
    t = jnp.arange(S)
    means = []
    for gi, w in enumerate(POOL_WINDOWS):
        lo = jnp.clip(t - w // 2, 0, S)
        hi = jnp.clip(t + w - w // 2, 0, S)
        total = csum[:, hi, gi] - csum[:, lo, gi]
        means.append(total / (hi - lo).astype(jnp.float32)[:, None])
    pooled = jnp.stack(means, axis=2)
    mixed = (pooled - ug.astype(jnp.float32)).astype(u.dtype)
    y = jnp.einsum('bsgc,gcd->bsgd', mixed, pool_w).reshape(B, S, POOL_WIDTH)
    return y * pool_scale

def _peer(h, w_query, sub_keys, u_table, v_table):
    B, S, D = h.shape
    q = (h @ w_query).reshape(B, S, PEER_HEADS, 2, PEER_HALF)
    scores = jnp.einsum('bshpc,hpnc->bshpn', q, sub_keys).astype(jnp.float32)
    top_s, top_i = lax.top_k(scores, PEER_TOPK)
    cand_s = (top_s[..., 0, :, None] + top_s[..., 1, None, :]).reshape(B, S, PEER_HEADS, PEER_TOPK * PEER_TOPK)
    cand_i = (top_i[..., 0, :, None] * N_KEYS + top_i[..., 1, None, :]).reshape(B, S, PEER_HEADS, PEER_TOPK * PEER_TOPK)
    best_s, best_pos = lax.top_k(cand_s, PEER_TOPK)
    expert_idx = jnp.take_along_axis(cand_i, best_pos, axis=-1)
    gate = jax.nn.softmax(best_s, axis=-1).astype(h.dtype)
    nc = (B * S) // PEER_CHUNK
    xs = h.reshape(nc, PEER_CHUNK, D)
    idx = expert_idx.reshape(nc, PEER_CHUNK, PEER_HEADS, PEER_TOPK)
    gs = gate.reshape(nc, PEER_CHUNK, PEER_HEADS, PEER_TOPK)

    def chunk(args):
        xc, ic, gc = args
        u_e = jnp.take(u_table, ic, axis=0)
        act = jax.nn.gelu(jnp.einsum('thkd,td->thk', u_e, xc), approximate=False) * gc
        v_e = jnp.take(v_table, ic, axis=0)
        return jnp.einsum('thk,thkd->td', act, v_e)

    return lax.map(chunk, (xs, idx, gs)).reshape(B, S, D)

def setup_inputs(seed: int = 0) -> dict:
    key = jax.random.key(seed)
    ks = jax.random.split(key, 17)
    nrm = lambda k, shape, s: jax.random.normal(k, shape, jnp.float32) * s
    L = DEPTH
    return {
        "x": nrm(ks[0], (BATCH, SEQ, D_MODEL), 1.0),
        "norm1_g": 1.0 + nrm(ks[1], (L, D_MODEL), 0.01),
        "w_in": nrm(ks[2], (L, D_MODEL, IN_WIDTH), D_MODEL ** -0.5),
        "sink_logits": nrm(ks[3], (L, N_Q_HEADS), 0.5),
        "pool_w": nrm(ks[4], (L, POOL_GROUPS, POOL_GROUP_DIM, POOL_GROUP_DIM), POOL_GROUP_DIM ** -0.5),
        "pool_scale": 1.0 + nrm(ks[5], (L, POOL_WIDTH), 0.1),
        "w_branch": nrm(ks[6], (L, N_BRANCHES, ATTN_WIDTH, D_MODEL), ATTN_WIDTH ** -0.5),
        "w_gate": nrm(ks[7], (L, D_MODEL, N_BRANCHES * D_MODEL), D_MODEL ** -0.5),
        "b_gate": nrm(ks[8], (L, N_BRANCHES * D_MODEL), 0.01),
        "w_out": nrm(ks[9], (L, D_MODEL, D_MODEL), D_MODEL ** -0.5),
        "norm2_g": 1.0 + nrm(ks[10], (L, D_MODEL), 0.01),
        "peer_w_query": nrm(ks[11], (L, D_MODEL, PEER_HEADS * PEER_QUERY_DIM), D_MODEL ** -0.5),
        "peer_sub_keys": nrm(ks[12], (L, PEER_HEADS, 2, N_KEYS, PEER_HALF), PEER_HALF ** -0.5),
        "peer_u": nrm(ks[13], (L, N_EXPERTS, D_MODEL), D_MODEL ** -0.5),
        "peer_v": nrm(ks[14], (L, N_EXPERTS, D_MODEL), 0.5),
        "norm_final_g": 1.0 + nrm(ks[15], (D_MODEL,), 0.01),
    }

def reference(x, norm1_g, w_in, sink_logits, pool_w, pool_scale, w_branch, w_gate, b_gate, w_out,
              norm2_g, peer_w_query, peer_sub_keys, peer_u, peer_v, norm_final_g):
    B, S, D = x.shape
    for l in range(DEPTH):
        h = _rmsnorm(x, norm1_g[l])
        proj = h @ w_in[l]
        q, k, v, u = jnp.split(proj, [ATTN_WIDTH, ATTN_WIDTH + KV_WIDTH, ATTN_WIDTH + 2 * KV_WIDTH], axis=-1)
        o_attn = _windowed_gqa(q, k, v, sink_logits[l])
        o_pool = _pool_mixer(u, pool_w[l], pool_scale[l])
        gates = jax.nn.sigmoid((h @ w_gate[l] + b_gate[l]).astype(jnp.float32)).astype(x.dtype)
        gates = gates.reshape(B, S, N_BRANCHES, D)
        merged = gates[:, :, 0] * (o_attn @ w_branch[l, 0]) + gates[:, :, 1] * (o_pool @ w_branch[l, 1])
        x = x + merged @ w_out[l]
        h2 = _rmsnorm(x, norm2_g[l])
        x = x + _peer(h2, peer_w_query[l], peer_sub_keys[l], peer_u[l], peer_v[l])
    return _rmsnorm(x, norm_final_g)


_drawn_inputs = setup_inputs


def setup_inputs(seed=0):
    import zlib

    import numpy as np

    out = dict(_drawn_inputs(seed))
    spreads = {}
    factors = {'norm1_g': 3.112,
     'sink_logits': 23.904,
     'b_gate': 19.21,
     'norm_final_g': 32.817,
     'norm2_g': 5.43}
    for name, (base, spread) in spreads.items():
        noise = np.random.default_rng([zlib.crc32(name.encode()), seed]).standard_normal(out[name].shape)
        drawn = base * np.exp(spread * noise) if base else spread * noise
        out[name] = __import__('jax').numpy.asarray(drawn.astype(out[name].dtype))
    for name, factor in factors.items():
        out[name] = (out[name] * factor).astype(out[name].dtype)
    return out
```

```python
from contextlib import ExitStack

import concourse.bass as bass
from concourse import mybir

F32 = mybir.dt.float32
U32 = mybir.dt.uint32
ALU = mybir.AluOpType
ACT = mybir.ActivationFunctionType
AX = mybir.AxisListType

P = 128
EPS = 1e-6
LOWEST = -3.4028234663852886e38
HEAD_DIM = 64
QH = 8
KVH = 2
GROUPS = 4
PEER_HEADS = 8
TOPK = 16
N_KEYS = 128
BANK = 512
RING = 8
ROUTE_STEPS = 21


class Steps:

    def __init__(self, sem, per):
        self.sem, self.per, self.base, self.n = sem, per, 0, 0

    def begin(self, t):
        self.base, self.n = t * self.per, 0

    def add(self, instruction):
        self.n += 1
        assert self.n <= self.per
        return instruction.then_inc(self.sem, 1)

    def wait(self, engine):
        engine.wait_ge(self.sem, self.base + self.n)


def settle(engine, passed):
    engine.sem_inc(passed, 1)


def after(engine, sem, value):
    if not (isinstance(value, int) and value <= 0):
        engine.wait_ge(sem, value)


def every_tile(engine, tiles, body):
    body(0)
    with engine.Fori(1, tiles) as t:
        body(t)


class Ring:

    def __init__(self, banks, full, free, per):
        assert per % len(banks) == 0
        self.banks, self.full, self.free, self.per = banks, full, free, per

    def open(self, engine):
        engine.sem_inc(self.free, len(self.banks))

    def bank(self, k):
        return self.banks[k % len(self.banks)]

    def claim(self, engine, t, k):
        engine.wait_ge(self.free, t * self.per + k + 1)
        return self.bank(k)

    def filled(self, engine, t, k):
        after(engine, self.full, t * self.per + k + 1)
        return self.bank(k)

    def emptied(self, engine, t, k):
        engine.wait_ge(self.free, t * self.per + k + 1 + len(self.banks))


def encoder_block(nc, x, norm1_g, w_in, sink_logits, pool_w, pool_scale, w_branch, w_gate, b_gate,
                  w_out, norm2_g, w_query, sub_keys_t, peer_u, peer_v, norm_final_g,
                  identity, band, bias_table, iota16, out):
    S, D = x.shape
    TILES = S // P
    KC = D // P
    ATT = QH * HEAD_DIM
    KVW = KVH * HEAD_DIM
    PW = D // 2
    AC = ATT // P
    CW = 3 * P
    BW = QH * CW + GROUPS
    SETS = PEER_HEADS * 2
    HK = PEER_HEADS * TOPK

    qT_d = nc.dram_tensor("qT_scratch", (S, ATT), F32, kind="Internal").ap()
    kT_d = nc.dram_tensor("kT_scratch", (S + 2 * P, P), F32, kind="Internal").ap()
    v_d = nc.dram_tensor("v_scratch", (S + 2 * P, KVW), F32, kind="Internal").ap()
    u_d = nc.dram_tensor("u_scratch", (S + 2 * P, PW), F32, kind="Internal").ap()
    gate_d = nc.dram_tensor("gate_scratch", (S, 2 * D), F32, kind="Internal").ap()
    x1_d = nc.dram_tensor("x1_scratch", (S, D), F32, kind="Internal").ap()
    h2_d = nc.dram_tensor("h2_scratch", (S, D), F32, kind="Internal").ap()
    h2T_d = nc.dram_tensor("h2T_scratch", (S, D), F32, kind="Internal").ap()

    def rows(t, n=1):
        return bass.ds(t * P, n * P)

    with ExitStack() as ctx:
        def sem(name):
            return ctx.enter_context(nc.semaphore(name))

        psum = [ctx.enter_context(nc.psum_tensor(f"bank{i}", [P, BANK], F32)) for i in range(8)]

        def keep(name, shape, dt=F32):
            return ctx.enter_context(nc.sbuf_tensor(name, shape, dt))

        ident = keep("ident", [P, P])
        gain = keep("gain", [P, D])
        small = keep("small", [P, 16])

        region1 = keep("region1", [P, 10240])
        chosen = region1[:, RING * D:RING * D + TILES * HK].bitcast(U32)
        weight = region1[:, RING * D + TILES * HK:RING * D + 2 * TILES * HK]
        region2 = keep("region2", [P, 16384])
        region3 = keep("region3", [P, 16384])

        def carve(region):
            at = [0]

            def take(n, dt=F32):
                at[0] += n
                assert at[0] <= region.shape[1], at
                return region[:, at[0] - n:at[0]] if dt is F32 else region[:, at[0] - n:at[0]].bitcast(dt)
            return take

        win_sb = region1[:, 0:KC * 1280].rearrange("p (k n) -> p k n", k=KC)
        wg_sb = region2[:, :].rearrange("p (k n) -> p k n", k=KC)
        wb_sb = region3[:, 0:2 * AC * D].rearrange("p (b k n) -> p b k n", b=2, k=AC)
        wo_sb = region3[:, 2 * AC * D:].rearrange("p (k n) -> p k n", k=KC)
        wq_sb = region2[:, :].rearrange("p (k n) -> p k n", k=KC)

        const_in = sem("const_in")
        win_in = sem("win_in")
        wg_in = sem("wg_in")
        wbo_in = sem("wbo_in")
        wq_in = sem("wq_in")
        eps_ready = sem("eps_ready")
        passed = sem("waits_passed")

        with ExitStack() as pctx:
            def tmp(name, shape, dt=F32):
                return pctx.enter_context(nc.sbuf_tensor(name, shape, dt))
            xin = tmp("xin", [P, D])
            h = tmp("h", [P, D])
            hT = tmp("hT", [P, KC, P])
            gates = region3[:, 0:2 * D]
            bg = region3[:, 2 * D:4 * D]
            q_sb = tmp("q_sb", [P, ATT])
            k_sb = tmp("k_sb", [P, P])
            v_sb = tmp("v_sb", [P, KVW])
            u_sb = tmp("u_sb", [P, PW])
            qT = tmp("qT_out", [P, ATT])
            kT = tmp("kT_out", [P, P])
            x_in = sem("x_in")
            sumsq_ready = sem("sumsq_ready")
            rms_ready = sem("rms_ready")
            rstd_ready = sem("rstd_ready")
            h_ready = sem("h_ready")
            by_act = Ring(psum[0:2], sem("project_act_full"), sem("project_act_free"), 6)
            by_dve = Ring(psum[2:7], sem("project_dve_full"), sem("project_dve_free"), 5)
            v_ready = sem("v_ready")
            gate_ready = sem("gate_ready")
            zero_ready = sem("zero_ready")
            pads_out = sem("pads_out")
            qT_out, kT_out, v_out, u_out, g_out = (
                sem(n) for n in ("qT_stored", "kT_stored", "v_stored", "u_stored", "gates_stored"))
            HT, Q, KV, QT, KT = 0, 2, 3, 4, 5
            U, G = 0, 1
            GCH = 2 * D // BANK

            with nc.Block() as block:
                @block.sync
                def _(sp):
                    sp.dma_start(xin[:, :], x[0:P, :]).then_inc(x_in, 16)
                    sp.dma_start(ident[:, :], identity).then_inc(const_in, 16)
                    sp.dma_start(gain[:, :], norm1_g.partition_broadcast(P)).then_inc(const_in, 16)
                    sp.dma_start(win_sb, w_in.rearrange("(k p) n -> p k n", p=P)).then_inc(win_in, 16)
                    sp.dma_start(bg, b_gate.partition_broadcast(P)).then_inc(const_in, 16)
                    sp.dma_start(wg_sb, w_gate.rearrange("(k p) n -> p k n", p=P)).then_inc(wg_in, 16)
                    with sp.Fori(1, TILES) as t:
                        sp.wait_ge(h_ready, t)
                        sp.dma_start(xin[:, :], x[rows(t), :]).then_inc(x_in, 16)
                    sp.wait_ge(g_out, 16 * TILES)
                    for b in range(2):
                        sp.dma_start(wb_sb[:, b, :, :], w_branch[b * ATT:(b + 1) * ATT, :].rearrange(
                            "(k p) n -> p k n", p=P)).then_inc(wbo_in, 16)
                    sp.dma_start(wo_sb, w_out.rearrange("(k p) n -> p k n", p=P)).then_inc(wbo_in, 16)

                @block.gpsimd
                def _(pool):
                    nc.gpsimd.memset(u_sb[:, :], 0.0).then_inc(zero_ready, 1)
                    pool.wait_ge(zero_ready, 1)
                    for at in (0, S + P):
                        pool.dma_start(kT_d[at:at + P, :], u_sb[:, 0:P]).then_inc(pads_out, 16)
                        pool.dma_start(v_d[at:at + P, :], u_sb[:, 0:KVW]).then_inc(pads_out, 16)
                        pool.dma_start(u_d[at:at + P, :], u_sb[:, :]).then_inc(pads_out, 16)
                    pool.wait_ge(pads_out, 6 * 16)
                    nc.gpsimd.memset(small[:, 12:13], 0.0).then_inc(zero_ready, 1)
                    with pool.Fori(0, TILES) as t:
                        pool.wait_ge(v_ready, t + 1)
                        settle(pool, passed)
                        pool.dma_start(v_d[rows(t + 1), :], v_sb[:, :]).then_inc(v_out, 16)
                        by_dve.emptied(pool, t, U)
                        settle(pool, passed)
                        pool.dma_start(u_d[rows(t + 1), :], u_sb[:, :]).then_inc(u_out, 16)
                        by_act.emptied(pool, t, QT)
                        settle(pool, passed)
                        pool.dma_start(qT_d[rows(t), :], qT[:, :]).then_inc(qT_out, 16)
                        by_act.emptied(pool, t, KT)
                        settle(pool, passed)
                        pool.dma_start(kT_d[rows(t + 1), :], kT[:, :]).then_inc(kT_out, 16)
                        pool.wait_ge(gate_ready, t + 1)
                        settle(pool, passed)
                        pool.dma_start(gate_d[rows(t), :], gates).then_inc(g_out, 16)
                    for stored in (qT_out, kT_out, v_out, u_out, g_out):
                        pool.wait_ge(stored, 16 * TILES)

                @block.scalar
                def _(act):
                    by_act.open(act)
                    act.wait_ge(eps_ready, 1)
                    def body(t):
                        act.wait_ge(x_in, 16 * t + 16)
                        after(act, rstd_ready, t)
                        nc.scalar.activation(h[:, :], xin[:, :], ACT.Square, accum_out=small[:, 0:1]
                                             ).then_inc(sumsq_ready, 1)
                        act.wait_ge(sumsq_ready, t + 1)
                        nc.scalar.activation(small[:, 1:2], small[:, 0:1], ACT.Sqrt, bias=small[:, 14:15],
                                             scale=1.0 / D).then_inc(rms_ready, 1)
                        by_dve.filled(act, t, -1)
                        for half in range(2):
                            bank = by_act.filled(act, t, HT + half)
                            nc.scalar.activation(hT[:, 4 * half:4 * half + 4, :],
                                                 bank[:, :].rearrange("p (k n) -> p k n", k=4),
                                                 ACT.Copy).then_inc(by_act.free, 1)
                        bank = by_act.filled(act, t, Q)
                        nc.scalar.activation(q_sb[:, :].rearrange("p (c g d) -> p g c d", c=4, g=KVH),
                                             bank[:, :].rearrange("p (g c d) -> p g c d", g=KVH, c=4),
                                             ACT.Copy).then_inc(by_act.free, 1)
                        bank = by_act.filled(act, t, KV)
                        after(act, v_out, 16 * t)
                        nc.scalar.activation(v_sb[:, :], bank[:, P:P + KVW], ACT.Copy).then_inc(v_ready, 1)
                        nc.scalar.activation(k_sb[:, :], bank[:, 0:P], ACT.Copy).then_inc(by_act.free, 1)
                        bank = by_act.filled(act, t, QT)
                        after(act, qT_out, 16 * t)
                        nc.scalar.activation(qT[:, :], bank[:, :], ACT.Copy).then_inc(by_act.free, 1)
                        bank = by_act.filled(act, t, KT)
                        after(act, kT_out, 16 * t)
                        nc.scalar.activation(kT[:, :], bank[:, 0:P], ACT.Copy).then_inc(by_act.free, 1)
                        by_dve.emptied(act, t, G + GCH - 1)
                        nc.scalar.activation(gates, gates, ACT.Sigmoid).then_inc(gate_ready, 1)

                    every_tile(act, TILES, body)

                @block.vector
                def _(dve):
                    by_dve.open(dve)
                    nc.vector.memset(small[:, 14:15], EPS).then_inc(eps_ready, 1)
                    dve.wait_ge(const_in, 48)
                    dve.wait_ge(zero_ready, 2)
                    def body(t):
                        dve.wait_ge(rms_ready, t + 1)
                        nc.vector.reciprocal(small[:, 2:3], small[:, 1:2]).then_inc(rstd_ready, 1)
                        dve.wait_ge(rstd_ready, t + 1)
                        nc.vector.scalar_tensor_tensor(out=h[:, :], in0=xin[:, :], scalar=small[:, 2:3],
                                                       in1=gain[:, :], op0=ALU.mult, op1=ALU.mult
                                                       ).then_inc(h_ready, 1)
                        bank = by_dve.filled(dve, t, U)
                        after(dve, u_out, 16 * t)
                        nc.vector.tensor_copy(u_sb[:, :], bank[:, :]).then_inc(by_dve.free, 1)
                        after(dve, g_out, 16 * t)
                        for c in range(GCH):
                            bank = by_dve.filled(dve, t, G + c)
                            part = slice(c * BANK, (c + 1) * BANK)
                            nc.vector.tensor_tensor(gates[:, part], bank[:, :], bg[:, part], ALU.add
                                                    ).then_inc(by_dve.free, 1)

                    every_tile(dve, TILES, body)

                @block.tensor
                def _(pe):
                    def project(t, ring, use, w, n):
                        bank = ring.claim(pe, t, use)
                        for k in range(KC):
                            last = nc.tensor.matmul(bank[:, 0:n], hT[:, k, :], w[:, k, :],
                                                    start=(k == 0), stop=(k == KC - 1))
                        last.then_inc(ring.full, 1)

                    pe.wait_ge(const_in, 48)
                    with pe.Fori(0, TILES) as t:
                        pe.wait_ge(h_ready, t + 1)
                        for half in range(2):
                            bank = by_act.claim(pe, t, HT + half)
                            for k in range(4):
                                c = (4 * half + k) * P
                                last = nc.tensor.transpose(bank[:, k * P:(k + 1) * P], h[:, c:c + P], ident[:, :])
                            last.then_inc(by_act.full, 1)
                        by_act.emptied(pe, t, HT + 1)
                        pe.wait_ge(win_in, 16)
                        project(t, by_act, Q, win_sb[:, :, 0:ATT], ATT)
                        project(t, by_act, KV, win_sb[:, :, ATT:ATT + 2 * KVW], 2 * KVW)
                        project(t, by_dve, U, win_sb[:, :, ATT + 2 * KVW:], PW)
                        bank = by_act.claim(pe, t, QT)
                        for c in range(AC):
                            last = nc.tensor.transpose(bank[:, c * P:(c + 1) * P], q_sb[:, c * P:(c + 1) * P],
                                                       ident[:, :])
                        last.then_inc(by_act.full, 1)
                        bank = by_act.claim(pe, t, KT)
                        nc.tensor.transpose(bank[:, 0:P], k_sb[:, :], ident[:, :]).then_inc(by_act.full, 1)
                        pe.wait_ge(wg_in, 16)
                        for c in range(GCH):
                            project(t, by_dve, G + c, wg_sb[:, :, c * BANK:(c + 1) * BANK], BANK)

        with ExitStack() as mctx:
            def tmp(name, shape, dt=F32):
                return mctx.enter_context(nc.sbuf_tensor(name, shape, dt))
            take = carve(region1)
            bias = take(BW)
            L = bias[:, 0:QH * CW].rearrange("p (h c) -> p h c", h=QH)
            rcount = bias[:, QH * CW:BW]
            qT = take(ATT).rearrange("p (c n) -> p c n", c=4)
            kw = take(CW).rearrange("p (b n) -> p b n", b=3)
            vw = take(3 * KVW).rearrange("p (b n) -> p b n", b=3)
            uw = take(3 * PW).rearrange("p (b n) -> p b n", b=3)
            PT = take(2 * CW).rearrange("p (s b n) -> p s b n", s=2, b=3)
            o_sb = take(ATT)
            oT = take(ATT).rearrange("p (k n) -> p k n", k=AC)
            mixed = take(PW)
            mixedT = take(PW).rearrange("p (g n) -> p g n", g=GROUPS)
            opT = take(PW).rearrange("p (k n) -> p k n", k=AC)
            gates = tmp("gates_in", [P, 2 * D])
            xres = tmp("xres", [P, D])
            h2 = tmp("h2_new", [P, D])[:, :]
            mT = tmp("mT", [P, KC, P])
            x1 = tmp("x1", [P, D])
            h2T = tmp("h2T_out", [P, D])
            band_sb = tmp("band_sb", [P, 3, GROUPS, P])
            pw_sb = take(GROUPS * P).rearrange("p (g n) -> p g n", g=GROUPS)
            ps_sb = tmp("ps_sb", [P, GROUPS])
            sink = tmp("sink", [P, QH])
            nsink = tmp("nsink", [P, QH])
            nmax = tmp("nmax", [P, QH])
            nshift = tmp("nshift", [P, QH])
            sdiff = tmp("sdiff", [P, QH])
            sexp = tmp("sexp", [P, QH])
            rsum = tmp("rsum", [P, QH])
            den = tmp("den", [P, QH])
            rden = tmp("rden", [P, QH])
            mconst_in, nsink_ready = sem("mix_const_in"), sem("nsink_ready")
            bias_in, qk_in, vu_in, gx_in = sem("bias_in"), sem("qk_in"), sem("vu_in"), sem("gx_in")
            shift_ready, exp_ready = sem("shift_ready"), sem("exp_ready")
            rden_ready, pv_done = sem("rden_ready"), sem("pv_done")
            softmax = Steps(sem("softmax_steps"), 4)
            merged_ready = sem("merged_ready")
            sumsq_ready, rms_ready, rstd_ready, h2_ready = (
                sem(n) for n in ("sumsq1_ready", "rms1_ready", "rstd1_ready", "h2_ready"))
            x1_out, h2_out, h2T_out = sem("x1_stored"), sem("h2_stored"), sem("h2T_stored")
            a_dve = Ring(psum[0:2], sem("a_dve_full"), sem("a_dve_free"), 12)
            a_act = Ring(psum[2:4], sem("a_act_full"), sem("a_act_free"), 10)
            b_dve = Ring(psum[4:6], sem("b_dve_full"), sem("b_dve_free"), 6)
            b_act = Ring(psum[6:8], sem("b_act_full"), sem("b_act_free"), 4)
            LOGITS, POOLED, ATTN, MIXED = 0, 8, 9, 10
            PTR, OT, MIXEDT = 0, 8, 9
            BRANCH, OUT = 0, 4
            MT, H2T = 0, 2
            EXPS = QH + 1

            def pipeline(engine, attend, merge, finish, norm):
                def both(t):
                    attend(t)
                    merge(t - 1)
                    finish(t)
                    norm(t - 1)

                attend(0)
                finish(0)
                both(1)
                with engine.Fori(2, TILES) as t:
                    both(t)
                merge(TILES - 1)
                norm(TILES - 1)

            with nc.Block() as block:
                @block.sync
                def _(sp):
                    sp.dma_start(wq_sb, w_query.rearrange("(k p) n -> p k n", p=P)).then_inc(wq_in, 16)
                    sp.dma_start(gain[:, :], norm2_g.partition_broadcast(P)).then_inc(mconst_in, 16)

                    def attend(t, first=False):
                        if not first:
                            a_act.filled(sp, t - 1, PTR + QH - 1)
                            a_dve.emptied(sp, t - 1, POOLED)
                        sp.dma_start(bias, bias_table[rows(t), :]).then_inc(bias_in, 16)
                        sp.dma_start(qT, qT_d[rows(t), :].rearrange("p (c n) -> p c n", c=4)).then_inc(qk_in, 16)
                        sp.dma_start(kw, kT_d[rows(t, 3), :].rearrange("(b p) n -> p b n", p=P)).then_inc(qk_in, 16)
                        if not first:
                            a_dve.filled(sp, t - 1, ATTN)
                        sp.dma_start(vw, v_d[rows(t, 3), :].rearrange("(b p) n -> p b n", p=P)).then_inc(vu_in, 16)
                        sp.dma_start(uw, u_d[rows(t, 3), :].rearrange("(b p) n -> p b n", p=P)).then_inc(vu_in, 16)

                    def merge(t, first=False):
                        if not first:
                            b_dve.emptied(sp, t - 1, OUT + 1)
                            b_act.filled(sp, t - 1, MT + 1)
                        sp.dma_start(gates[:, :], gate_d[rows(t), :]).then_inc(gx_in, 16)
                        sp.dma_start(xres[:, :], x[rows(t), :]).then_inc(gx_in, 16)

                    attend(0, True)
                    merge(0, True)
                    sp.dma_start(band_sb[:, :, :, :], band).then_inc(mconst_in, 16)
                    sp.dma_start(pw_sb, pool_w.rearrange("g c d -> c g d")).then_inc(mconst_in, 16)
                    sp.dma_start(ps_sb[:, :], pool_scale).then_inc(mconst_in, 16)
                    sp.dma_start(sink[:, :], sink_logits.partition_broadcast(P)).then_inc(mconst_in, 16)
                    with sp.Fori(1, TILES) as t:
                        attend(t)
                        merge(t)

                @block.gpsimd
                def _(pool):
                    with pool.Fori(0, TILES) as t:
                        b_dve.emptied(pool, t, OUT + 1)
                        settle(pool, passed)
                        pool.dma_start(x1_d[rows(t), :], x1[:, :]).then_inc(x1_out, 16)
                        pool.wait_ge(h2_ready, t + 1)
                        settle(pool, passed)
                        pool.dma_start(h2_d[rows(t), :], h2).then_inc(h2_out, 16)
                        b_act.emptied(pool, t, H2T + 1)
                        settle(pool, passed)
                        pool.dma_start(h2T_d[rows(t), :], h2T[:, :]).then_inc(h2T_out, 16)
                    for stored in (x1_out, h2_out, h2T_out):
                        pool.wait_ge(stored, 16 * TILES)

                @block.tensor
                def _(pe):
                    def attend(t):
                        pe.wait_ge(qk_in, 32 * t + 32)
                        for hd in range(QH):
                            g, c = divmod(hd, 4)
                            half = slice(g * HEAD_DIM, (g + 1) * HEAD_DIM)
                            bank = a_dve.claim(pe, t, LOGITS + hd)
                            nc.tensor.matmul(bank[:, 0:CW], qT[half, c, :],
                                             kw[half, :, :].rearrange("p b n -> p (b n)"), start=True, stop=True
                                             ).then_inc(a_dve.full, 1)
                        pe.wait_ge(vu_in, 32 * t + 32)
                        bank = a_dve.claim(pe, t, POOLED)
                        for g in range(GROUPS):
                            for b in range(3):
                                last = nc.tensor.matmul(bank[:, g * P:(g + 1) * P], band_sb[:, b, g, :],
                                                        uw[:, b, g * P:(g + 1) * P], start=(b == 0), stop=(b == 2))
                        last.then_inc(a_dve.full, 1)

                        def weigh(hd):
                            a_act.emptied(pe, t, PTR + hd)
                            g = hd // 4
                            for b in range(3):
                                last = nc.tensor.matmul(a_dve.bank(ATTN)[:, hd * HEAD_DIM:(hd + 1) * HEAD_DIM],
                                                        PT[:, hd % 2, b, :],
                                                        vw[:, b, g * HEAD_DIM:(g + 1) * HEAD_DIM],
                                                        start=(b == 0), stop=(b == 2))
                            last.then_inc(pv_done if hd < QH - 1 else a_dve.full, 1)

                        a_dve.claim(pe, t, ATTN)
                        for hd in range(QH):
                            pe.wait_ge(exp_ready, EXPS * t + hd + 1)
                            bank = a_act.claim(pe, t, PTR + hd)
                            for b in range(3):
                                last = nc.tensor.transpose(bank[:, b * P:(b + 1) * P], L[:, hd, b * P:(b + 1) * P],
                                                           ident[:, :])
                            last.then_inc(a_act.full, 1)
                            if hd:
                                weigh(hd - 1)
                        weigh(QH - 1)

                    def finish(t):
                        a_dve.emptied(pe, t, POOLED)
                        a_dve.emptied(pe, t, ATTN)
                        for use, rows_of in ((OT, o_sb), (MIXEDT, mixed)):
                            bank = a_act.claim(pe, t, use)
                            for c in range(AC):
                                last = nc.tensor.transpose(bank[:, c * P:(c + 1) * P], rows_of[:, c * P:(c + 1) * P],
                                                           ident[:, :])
                            last.then_inc(a_act.full, 1)
                        a_act.emptied(pe, t, MIXEDT)
                        for two in range(2):
                            bank = a_dve.claim(pe, t, MIXED + two)
                            for i in range(2):
                                g = 2 * two + i
                                last = nc.tensor.matmul(bank[:, i * P:(i + 1) * P], pw_sb[:, g, :], mixedT[:, g, :],
                                                        start=True, stop=True)
                            last.then_inc(a_dve.full, 1)

                    def merge(t):
                        a_act.emptied(pe, t, OT)
                        a_dve.emptied(pe, t, MIXED + 1)
                        for c in range(2):
                            for b, of in enumerate((oT, opT)):
                                bank = b_dve.claim(pe, t, BRANCH + 2 * c + b)
                                for k in range(AC):
                                    last = nc.tensor.matmul(bank[:, :], of[:, k, :],
                                                            wb_sb[:, b, k, c * BANK:(c + 1) * BANK],
                                                            start=(k == 0), stop=(k == AC - 1))
                                last.then_inc(b_dve.full, 1)
                        for c in range(2):
                            pe.wait_ge(merged_ready, 2 * t + c + 1)
                            bank = b_act.claim(pe, t, MT + c)
                            for k in range(4):
                                at = c * BANK + k * P
                                last = nc.tensor.transpose(bank[:, k * P:(k + 1) * P], gates[:, at:at + P], ident[:, :])
                            last.then_inc(b_act.full, 1)
                        b_act.emptied(pe, t, MT + 1)
                        for c in range(2):
                            bank = b_dve.claim(pe, t, OUT + c)
                            for k in range(KC):
                                last = nc.tensor.matmul(bank[:, :], mT[:, k, :], wo_sb[:, k, c * BANK:(c + 1) * BANK],
                                                        start=(k == 0), stop=(k == KC - 1))
                            last.then_inc(b_dve.full, 1)

                    def norm(t):
                        pe.wait_ge(h2_ready, t + 1)
                        for c in range(2):
                            bank = b_act.claim(pe, t, H2T + c)
                            for k in range(4):
                                at = c * BANK + k * P
                                last = nc.tensor.transpose(bank[:, k * P:(k + 1) * P], h2[:, at:at + P], ident[:, :])
                            last.then_inc(b_act.full, 1)

                    pe.wait_ge(mconst_in, 80)
                    pe.wait_ge(wbo_in, 48)
                    pipeline(pe, attend, merge, finish, norm)

                @block.scalar
                def _(act):
                    def attend(t):
                        act.wait_ge(shift_ready, 2 * t + 2)
                        for hd in range(QH):
                            nc.scalar.activation(L[:, hd, :], L[:, hd, :], ACT.Exp, bias=nshift[:, hd:hd + 1],
                                                 accum_out=rsum[:, hd:hd + 1]).then_inc(exp_ready, 1)
                        nc.scalar.activation(sexp[:, :], sdiff[:, :], ACT.Exp).then_inc(exp_ready, 1)
                        for hd in range(QH):
                            bank = a_act.filled(act, t, PTR + hd)
                            if hd >= 2:
                                act.wait_ge(pv_done, (QH - 1) * t + hd - 1)
                            nc.scalar.activation(PT[:, hd % 2, :, :], bank[:, 0:CW].rearrange("p (b n) -> p b n", b=3),
                                                 ACT.Copy).then_inc(a_act.free, 1)

                    def finish(t):
                        for use, to in ((OT, oT), (MIXEDT, mixedT)):
                            bank = a_act.filled(act, t, use)
                            nc.scalar.activation(to, bank[:, :].rearrange("p (k n) -> p k n", k=AC),
                                                 ACT.Copy).then_inc(a_act.free, 1)

                    def merge(t):
                        for c in range(2):
                            bank = b_act.filled(act, t, MT + c)
                            nc.scalar.activation(mT[:, 4 * c:4 * c + 4, :], bank[:, :].rearrange("p (k n) -> p k n", k=4),
                                                 ACT.Copy).then_inc(b_act.free, 1)
                        b_dve.emptied(act, t, OUT + 1)
                        after(act, h2_out, 16 * t)
                        nc.scalar.activation(h2, x1[:, :], ACT.Square, accum_out=small[:, 0:1]).then_inc(sumsq_ready, 1)
                        act.wait_ge(sumsq_ready, t + 1)
                        nc.scalar.activation(small[:, 1:2], small[:, 0:1], ACT.Sqrt, bias=small[:, 14:15],
                                             scale=1.0 / D).then_inc(rms_ready, 1)

                    def norm(t):
                        for c in range(2):
                            bank = b_act.filled(act, t, H2T + c)
                            if c == 0:
                                after(act, h2T_out, 16 * t)
                            nc.scalar.activation(h2T[:, c * BANK:(c + 1) * BANK], bank[:, :], ACT.Copy
                                                 ).then_inc(b_act.free, 1)

                    a_act.open(act)
                    b_act.open(act)
                    pipeline(act, attend, merge, finish, norm)

                @block.vector
                def _(dve):
                    def attend(t):
                        softmax.begin(t)
                        dve.wait_ge(bias_in, 16 * t + 16)
                        for hd in range(QH):
                            bank = a_dve.filled(dve, t, LOGITS + hd)
                            nc.vector.scalar_tensor_tensor(out=L[:, hd, :], in0=bank[:, 0:CW], scalar=HEAD_DIM ** -0.5,
                                                           in1=L[:, hd, :], op0=ALU.mult, op1=ALU.add
                                                           ).then_inc(a_dve.free, 1)
                        a_dve.emptied(dve, t, LOGITS + QH - 1)
                        softmax.add(nc.vector.reduce_max(nmax[:, :], L, AX.X, negate=True))
                        softmax.wait(dve)
                        nc.vector.tensor_tensor(nshift[:, :], nmax[:, :], nsink[:, :], ALU.min).then_inc(shift_ready, 1)
                        dve.wait_ge(shift_ready, 2 * t + 1)
                        nc.vector.tensor_tensor(sdiff[:, :], sink[:, :], nshift[:, :], ALU.add).then_inc(shift_ready, 1)
                        bank = a_dve.filled(dve, t, POOLED)
                        for g in range(GROUPS):
                            part = slice(g * P, (g + 1) * P)
                            last = nc.vector.scalar_tensor_tensor(out=mixed[:, part], in0=bank[:, part],
                                                                  scalar=rcount[:, g:g + 1], in1=uw[:, 1, part],
                                                                  op0=ALU.mult, op1=ALU.subtract)
                        last.then_inc(a_dve.free, 1)
                        dve.wait_ge(exp_ready, EXPS * (t + 1))
                        softmax.add(nc.vector.tensor_tensor(den[:, :], rsum[:, :], sexp[:, :], ALU.add))
                        softmax.wait(dve)
                        softmax.add(nc.vector.reciprocal(rden[:, :], den[:, :]))
                        softmax.wait(dve)
                        bank = a_dve.filled(dve, t, ATTN)
                        nc.vector.tensor_tensor(o_sb.rearrange("p (h d) -> p h d", h=QH),
                                                bank[:, :].rearrange("p (h d) -> p h d", h=QH),
                                                rden[:, :].unsqueeze(2).to_broadcast([P, QH, HEAD_DIM]), ALU.mult
                                                ).then_inc(a_dve.free, 1)
                        softmax.add(nc.vector.memset(small[:, 13:14], 0.0))

                    def finish(t):
                        for two in range(2):
                            bank = a_dve.filled(dve, t, MIXED + two)
                            nc.vector.tensor_tensor(opT[:, 2 * two:2 * two + 2, :],
                                                    bank[:, 0:2 * P].rearrange("p (g n) -> p g n", g=2),
                                                    ps_sb[:, 2 * two:2 * two + 2].unsqueeze(2).to_broadcast([P, 2, P]),
                                                    ALU.mult).then_inc(a_dve.free, 1)

                    def merge(t):
                        dve.wait_ge(gx_in, 32 * t + 32)
                        for c in range(2):
                            for b in range(2):
                                bank = b_dve.filled(dve, t, BRANCH + 2 * c + b)
                                part = gates[:, b * D + c * BANK:b * D + (c + 1) * BANK]
                                nc.vector.tensor_tensor(part, bank[:, :], part, ALU.mult).then_inc(b_dve.free, 1)
                            b_dve.emptied(dve, t, BRANCH + 2 * c + 1)
                            to = gates[:, c * BANK:(c + 1) * BANK]
                            nc.vector.tensor_tensor(to, to, gates[:, D + c * BANK:D + (c + 1) * BANK], ALU.add
                                                    ).then_inc(merged_ready, 1)
                        after(dve, x1_out, 16 * t)
                        for c in range(2):
                            bank = b_dve.filled(dve, t, OUT + c)
                            part = slice(c * BANK, (c + 1) * BANK)
                            nc.vector.tensor_tensor(x1[:, part], bank[:, :], xres[:, part], ALU.add
                                                    ).then_inc(b_dve.free, 1)
                        dve.wait_ge(rms_ready, t + 1)
                        nc.vector.reciprocal(small[:, 2:3], small[:, 1:2]).then_inc(rstd_ready, 1)
                        dve.wait_ge(rstd_ready, t + 1)
                        nc.vector.scalar_tensor_tensor(out=h2, in0=x1[:, :], scalar=small[:, 2:3], in1=gain[:, :],
                                                       op0=ALU.mult, op1=ALU.mult).then_inc(h2_ready, 1)

                    def norm(t):
                        pass

                    a_dve.open(dve)
                    b_dve.open(dve)
                    dve.wait_ge(mconst_in, 80)
                    nc.vector.tensor_scalar(nsink[:, :], sink[:, :], -1.0, None, ALU.mult).then_inc(nsink_ready, 1)
                    dve.wait_ge(nsink_ready, 1)
                    pipeline(dve, attend, merge, finish, norm)

        with ExitStack() as rctx:
            def tmp(name, shape, dt=F32):
                return rctx.enter_context(nc.sbuf_tensor(name, shape, dt))
            take = carve(region3)
            sk_sb = take(SETS * N_KEYS).rearrange("p (s n) -> p s n", s=SETS)
            q_sb = take(2 * D)
            qT = take(2 * D).rearrange("p (s n) -> p s n", s=SETS)
            scores = take(SETS * N_KEYS).rearrange("p (s n) -> p s n", s=SETS)
            cand = take(PEER_HEADS * TOPK * TOPK)
            cand3 = cand.rearrange("p (h n) -> p h n", h=PEER_HEADS)
            cand4 = cand.rearrange("p (h a b) -> p h a b", h=PEER_HEADS, a=TOPK)
            hit = take(HK * TOPK)
            hit4 = hit.rearrange("p (h k a) -> p h k a", h=PEER_HEADS, k=TOPK)
            hit3 = hit.rearrange("p (n a) -> p n a", a=TOPK)
            top = take(SETS * TOPK).rearrange("p (s k) -> p s k", s=SETS)
            topi = take(SETS * TOPK, U32).rearrange("p (s k) -> p s k", s=SETS)
            topf = take(SETS * TOPK).rearrange("p (s k) -> p s k", s=SETS)
            best = take(HK).rearrange("p (h k) -> p h k", h=PEER_HEADS)
            pos = take(HK, U32).rearrange("p (h k) -> p h k", h=PEER_HEADS)
            half_pos = take(2 * HK, U32).rearrange("p (i n) -> p i n", i=2)
            half_f = take(2 * HK).rearrange("p (i h k) -> p i h k", i=2, h=PEER_HEADS)
            found = take(2 * HK).rearrange("p (i n) -> p i n", i=2)
            shifted = tmp("shifted", [P, HK])
            wsum = tmp("wsum", [P, PEER_HEADS])
            rwsum = tmp("rwsum", [P, PEER_HEADS])
            iota_sb = tmp("iota_sb", [P, TOPK])
            h2T = tmp("h2T_in", [P, D])
            rconst_in, h2T_in = sem("route_const_in"), sem("h2T_in_sem")
            scores_used = sem("scores_used")
            shifted_ready, wexp_ready = sem("shifted_ready"), sem("wexp_ready")
            ring = Ring(psum[0:4], sem("route_full"), sem("route_free"), 12)
            QUERY, QUERYT, SCORE = 0, 4, 8
            topk = Steps(sem("topk_steps"), ROUTE_STEPS)

            with nc.Block() as block:
                @block.sync
                def _(sp):
                    sp.dma_start(h2T[:, :], h2T_d[0:P, :]).then_inc(h2T_in, 16)
                    sp.dma_start(sk_sb, sub_keys_t).then_inc(rconst_in, 16)
                    sp.dma_start(iota_sb[:, :], iota16).then_inc(rconst_in, 16)
                    with sp.Fori(1, TILES) as t:
                        ring.filled(sp, t - 1, QUERY + 3)
                        sp.dma_start(h2T[:, :], h2T_d[rows(t), :]).then_inc(h2T_in, 16)

                @block.tensor
                def _(pe):
                    pe.wait_ge(wq_in, 16)
                    pe.wait_ge(rconst_in, 32)
                    with pe.Fori(0, TILES) as t:
                        pe.wait_ge(h2T_in, 16 * t + 16)
                        for c in range(4):
                            bank = ring.claim(pe, t, QUERY + c)
                            for k in range(KC):
                                last = nc.tensor.matmul(bank[:, :], h2T[:, k * P:(k + 1) * P],
                                                        wq_sb[:, k, c * BANK:(c + 1) * BANK],
                                                        start=(k == 0), stop=(k == KC - 1))
                            last.then_inc(ring.full, 1)
                        for c in range(4):
                            bank = ring.claim(pe, t, QUERYT + c)
                            for i in range(4):
                                at = (4 * c + i) * P
                                last = nc.tensor.transpose(bank[:, i * P:(i + 1) * P], q_sb[:, at:at + P], ident[:, :])
                            last.then_inc(ring.full, 1)
                        for c in range(4):
                            bank = ring.claim(pe, t, SCORE + c)
                            for i in range(4):
                                s = 4 * c + i
                                last = nc.tensor.matmul(bank[:, i * P:(i + 1) * P], qT[:, s, :], sk_sb[:, s, :],
                                                        start=True, stop=True)
                            last.then_inc(ring.full, 1)

                @block.scalar
                def _(act):
                    def copy_out(t):
                        for use, to in ((QUERY, q_sb), (QUERYT, qT.rearrange("p s n -> p (s n)")),
                                        (SCORE, scores.rearrange("p s n -> p (s n)"))):
                            for c in range(4):
                                bank = ring.filled(act, t, use + c)
                                if use == SCORE and c == 0:
                                    after(act, scores_used, t)
                                nc.scalar.activation(to[:, c * BANK:(c + 1) * BANK], bank[:, :], ACT.Copy
                                                     ).then_inc(ring.free, 1)

                    def exps(t):
                        act.wait_ge(shifted_ready, t + 1)
                        nc.scalar.activation(shifted[:, :], shifted[:, :], ACT.Exp).then_inc(wexp_ready, 1)

                    ring.open(act)
                    copy_out(0)
                    with act.Fori(1, TILES) as t:
                        copy_out(t)
                        exps(t - 1)
                    exps(TILES - 1)

                @block.vector
                def _(dve):
                    def top16(sets, values, to, to_index, used=None):
                        settle(dve, passed)
                        for s in range(sets):
                            last = nc.vector.max(to[:, s, 0:8], values[:, s, :])
                        topk.add(last)
                        topk.wait(dve)
                        settle(dve, passed)
                        for s in range(sets):
                            last = nc.vector.max_index(to_index[:, s, 0:8], to[:, s, 0:8], values[:, s, :])
                        topk.add(last)
                        topk.wait(dve)
                        settle(dve, passed)
                        for s in range(sets):
                            last = nc.vector.match_replace(values[:, s, :], to[:, s, 0:8], values[:, s, :], LOWEST)
                        topk.add(last)
                        topk.wait(dve)
                        settle(dve, passed)
                        for s in range(sets):
                            last = nc.vector.max(to[:, s, 8:16], values[:, s, :])
                        topk.add(last)
                        topk.wait(dve)
                        settle(dve, passed)
                        for s in range(sets):
                            last = nc.vector.max_index(to_index[:, s, 8:16], to[:, s, 8:16], values[:, s, :])
                        last.then_inc(used, 1) if used is not None else topk.add(last)

                    with dve.Fori(0, TILES) as t:
                        topk.begin(t)
                        ring.emptied(dve, t, SCORE + 3)
                        top16(SETS, scores, top, topi, scores_used)
                        dve.wait_ge(scores_used, t + 1)
                        pairs = top.rearrange("p (h i) k -> p h i k", i=2)
                        nc.vector.tensor_copy(topf, topi)
                        topk.add(nc.vector.tensor_tensor(
                            cand4, pairs[:, :, 0, :].unsqueeze(3).to_broadcast([P, PEER_HEADS, TOPK, TOPK]),
                            pairs[:, :, 1, :].unsqueeze(2).to_broadcast([P, PEER_HEADS, TOPK, TOPK]), ALU.add))
                        topk.wait(dve)
                        top16(PEER_HEADS, cand3, best, pos)
                        topk.wait(dve)
                        nc.vector.tensor_tensor(shifted[:, :].rearrange("p (h k) -> p h k", h=PEER_HEADS), best,
                                                best[:, :, 0:1].to_broadcast([P, PEER_HEADS, TOPK]), ALU.subtract
                                                ).then_inc(shifted_ready, 1)
                        flat = pos.rearrange("p h k -> p (h k)")
                        nc.vector.tensor_scalar(half_pos[:, 0, :], flat, 4, None, ALU.logical_shift_right)
                        topk.add(nc.vector.tensor_scalar(half_pos[:, 1, :], flat, 15, None, ALU.bitwise_and))
                        topk.wait(dve)
                        topk.add(nc.vector.tensor_copy(half_f.rearrange("p i h k -> p (i h k)"),
                                                       half_pos.rearrange("p i n -> p (i n)")))
                        topk.wait(dve)
                        keys = topf.rearrange("p (h i) k -> p h i k", i=2)
                        for i in range(2):
                            topk.add(nc.vector.tensor_tensor(
                                hit3, half_f[:, i, :, :].rearrange("p h k -> p (h k)").unsqueeze(2).to_broadcast([P, HK, TOPK]),
                                iota_sb[:, :].unsqueeze(1).to_broadcast([P, HK, TOPK]), ALU.is_equal))
                            topk.wait(dve)
                            topk.add(nc.vector.tensor_tensor(
                                hit4, hit4, keys[:, :, i, :].unsqueeze(2).to_broadcast([P, PEER_HEADS, TOPK, TOPK]),
                                ALU.mult))
                            topk.wait(dve)
                            topk.add(nc.vector.reduce_sum(found[:, i, :], hit3, AX.X))
                            topk.wait(dve)
                        nc.vector.scalar_tensor_tensor(out=chosen[:, bass.ds(t * HK, HK)], in0=found[:, 0, :],
                                                       scalar=float(N_KEYS), in1=found[:, 1, :],
                                                       op0=ALU.mult, op1=ALU.add)
                        dve.wait_ge(wexp_ready, t + 1)
                        topk.add(nc.vector.reduce_sum(wsum[:, :], shifted[:, :].rearrange("p (h k) -> p h k", h=PEER_HEADS),
                                                      AX.X))
                        topk.wait(dve)
                        topk.add(nc.vector.reciprocal(rwsum[:, :], wsum[:, :]))
                        topk.wait(dve)
                        topk.add(nc.vector.tensor_tensor(
                            weight[:, bass.ds(t * HK, HK)].rearrange("p (h k) -> p h k", h=PEER_HEADS),
                            shifted[:, :].rearrange("p (h k) -> p h k", h=PEER_HEADS),
                            rwsum[:, :].unsqueeze(2).to_broadcast([P, PEER_HEADS, TOPK]), ALU.mult))
                        topk.wait(dve)
                        assert topk.n == topk.per, topk.n

        take = carve(region1)
        u_rows = take(RING * D).rearrange("p (s n) -> p s n", s=RING)
        take = carve(region3)
        v_rows = take(RING * D).rearrange("p (s n) -> p s n", s=RING)
        h2_next, h2_now, x1_now, x2, y = (take(D) for _ in range(5))
        take = carve(region2)
        DIAGS = 4
        diag = take(DIAGS * P).rearrange("p (s n) -> p s n", s=DIAGS)
        dots = take(2 * TOPK).rearrange("p (s k) -> p s k", s=2)
        gelu = take(2 * TOPK).rearrange("p (s k) -> p s k", s=2)
        coef = take(2 * TOPK).rearrange("p (s k) -> p s k", s=2)
        rowid = take(2 * TOPK, U32).rearrange("p (s k) -> p s k", s=2)
        u_in = [sem(f"u_rows_in{i}") for i in range(RING)]
        v_in = [sem(f"v_rows_in{i}") for i in range(RING)]
        u_used, v_used = sem("u_rows_used"), sem("v_rows_used")
        ids_ready, gelu_ready, coef_ready, diag_ready = (
            sem(n) for n in ("ids_ready", "gelu_ready", "coef_ready", "diag_ready"))
        h2n_in, x1n_in, h2_copied = sem("h2_next_in"), sem("x1_now_in"), sem("h2_copied")
        egain_in, x2_ready = sem("final_gain_in"), sem("x2_ready")
        sumsq_ready, rms_ready, rstd_ready = sem("sumsq2_ready"), sem("rms2_ready"), sem("rstd2_ready")
        y_ready, y_out = sem("y_ready"), sem("y_stored")
        acc = psum[0:2]

        def head_steps(engine, start, step, end):
            def body(t):
                start(t)
                with engine.Fori(0, PEER_HEADS // 2) as pair:
                    for s in range(2):
                        step(t, t * PEER_HEADS + pair * 2 + s, s)
                end(t)

            every_tile(engine, TILES, body)

        def nothing(t):
            pass

        with nc.Block() as block:
            @block.sync
            def _(sp):
                sp.dma_start(gain[:, :], norm_final_g.partition_broadcast(P)).then_inc(egain_in, 16)
                sp.dma_start(h2_next, h2_d[0:P, :]).then_inc(h2n_in, 16)
                sp.dma_start(x1_now, x1_d[0:P, :]).then_inc(x1n_in, 16)
                with sp.Fori(1, TILES) as t:
                    sp.wait_ge(h2_copied, t)
                    sp.dma_start(h2_next, h2_d[rows(t), :]).then_inc(h2n_in, 16)
                    sp.wait_ge(x2_ready, 2 * t)
                    sp.dma_start(x1_now, x1_d[rows(t), :]).then_inc(x1n_in, 16)
                    sp.wait_ge(y_ready, t)
                    sp.dma_start(out[rows(t - 1), :], y).then_inc(y_out, 16)
                sp.wait_ge(y_ready, TILES)
                sp.dma_start(out[S - P:S, :], y).then_inc(y_out, 16)
                sp.wait_ge(y_out, 16 * TILES)

            @block.gpsimd
            def _(pool):
                def step(t, g, s):
                    nc.gpsimd.tensor_copy(rowid[:, s, :], chosen[:, bass.ds(g * TOPK, TOPK)]).then_inc(ids_ready, 1)
                    pool.wait_ge(ids_ready, g + 1)
                    for table, ring_rows, arrived, used in ((peer_u, u_rows, u_in, u_used), (peer_v, v_rows, v_in, v_used)):
                        for j in range(TOPK):
                            slot = j % RING
                            pool.wait_ge(used, g * TOPK + j + 1)
                            settle(pool, passed)
                            pool.indirect_dma_start(ring_rows[:, slot, :], None, table[:, :],
                                                    bass.IndirectOffsetOnAxis(rowid[:, s, j:j + 1], 0)
                                                    ).then_inc(arrived[slot], 16)

                head_steps(pool, nothing, step, nothing)

            def slot_value(g, j):
                return 16 * (g * (TOPK // RING) + j // RING + 1)

            @block.vector
            def _(dve):
                def start(t):
                    dve.wait_ge(h2n_in, 16 * t + 16)
                    nc.vector.tensor_copy(h2_now, h2_next).then_inc(h2_copied, 1)
                    dve.wait_ge(h2_copied, t + 1)
                    settle(dve, passed)

                def step(t, g, s):
                    for j in range(TOPK):
                        slot = j % RING
                        dve.wait_ge(u_in[slot], slot_value(g, j))
                        nc.vector.tensor_tensor_reduce(out=u_rows[:, slot, :], in0=u_rows[:, slot, :], in1=h2_now,
                                                       scale=1.0, scalar=0.0, op0=ALU.mult, op1=ALU.add,
                                                       accum_out=dots[:, s, j:j + 1]).then_inc(u_used, 1)
                    dve.wait_ge(gelu_ready, g + 1)
                    nc.vector.tensor_tensor(coef[:, s, :], gelu[:, s, :], weight[:, bass.ds(g * TOPK, TOPK)], ALU.mult
                                            ).then_inc(coef_ready, 1)

                def end(t):
                    dve.wait_ge(v_used, RING + HK * (t + 1))
                    dve.wait_ge(x1n_in, 16 * t + 16)
                    after(dve, rstd_ready, t)
                    for c in range(2):
                        part = slice(c * BANK, (c + 1) * BANK)
                        nc.vector.tensor_tensor(x2[:, part], acc[c][:, :], x1_now[:, part], ALU.add).then_inc(x2_ready, 1)
                    dve.wait_ge(rms_ready, t + 1)
                    nc.vector.reciprocal(small[:, 2:3], small[:, 1:2]).then_inc(rstd_ready, 1)
                    dve.wait_ge(rstd_ready, t + 1)
                    nc.vector.scalar_tensor_tensor(out=y, in0=x2, scalar=small[:, 2:3], in1=gain[:, :],
                                                   op0=ALU.mult, op1=ALU.mult).then_inc(y_ready, 1)

                dve.sem_inc(u_used, RING)
                dve.wait_ge(egain_in, 16)
                head_steps(dve, start, step, end)

            @block.scalar
            def _(act):
                def step(t, g, s):
                    act.wait_ge(u_used, RING + TOPK * (g + 1))
                    nc.scalar.activation(gelu[:, s, :], dots[:, s, :], ACT.Gelu).then_inc(gelu_ready, 1)
                    act.wait_ge(coef_ready, g + 1)
                    for j in range(TOPK):
                        act.wait_ge(v_used, g * TOPK + j + 1 + RING - DIAGS)
                        nc.scalar.activation(diag[:, j % DIAGS, :], ident[:, :], ACT.Copy, scale=coef[:, s, j:j + 1]
                                             ).then_inc(diag_ready, 1)

                def end(t):
                    act.wait_ge(x2_ready, 2 * t + 2)
                    after(act, y_out, 16 * t)
                    nc.scalar.activation(y, x2, ACT.Square, accum_out=small[:, 0:1]).then_inc(sumsq_ready, 1)
                    act.wait_ge(sumsq_ready, t + 1)
                    nc.scalar.activation(small[:, 1:2], small[:, 0:1], ACT.Sqrt, bias=small[:, 14:15],
                                         scale=1.0 / D).then_inc(rms_ready, 1)

                head_steps(act, nothing, step, end)

            @block.tensor
            def _(pe):
                def step(t, g, s, first=False):
                    for j in range(TOPK):
                        slot = j % RING
                        pe.wait_ge(diag_ready, g * TOPK + j + 1)
                        pe.wait_ge(v_in[slot], slot_value(g, j))
                        for c in range(2):
                            last = nc.tensor.matmul(acc[c][:, :], diag[:, j % DIAGS, :],
                                                    v_rows[:, slot, c * BANK:(c + 1) * BANK],
                                                    start=(first and j == 0), stop=True, skip_group_check=True)
                        last.then_inc(v_used, 1)

                def tile(t):
                    after(pe, x2_ready, 2 * t)
                    for s in range(2):
                        step(t, t * PEER_HEADS + s, s, first=(s == 0))
                    with pe.Fori(1, PEER_HEADS // 2) as pair:
                        for s in range(2):
                            step(t, t * PEER_HEADS + pair * 2 + s, s)

                pe.sem_inc(v_used, RING)
                every_tile(pe, TILES, tile)


_INS = ["x", "norm1_g", "w_in", "sink_logits", "pool_w", "pool_scale", "w_branch", "w_gate", "b_gate", "w_out",
        "norm2_g", "peer_w_query", "peer_sub_keys", "peer_u", "peer_v", "norm_final_g"]


def _constants(S):
    import numpy as np
    q, c = np.arange(P)[:, None], np.arange(3 * P)[None, :]
    dist = np.abs(q + P - c).astype(np.float32)
    slopes = np.array([2.0 ** (-8.0 * (h + 1) / QH) for h in range(QH)], np.float32)
    tiles = S // P
    windows = (2, 4, 8, 16)
    table = np.zeros((tiles, P, QH * 3 * P + GROUPS), np.float32)
    for t in range(tiles):
        s_abs = (t - 1) * P + c
        valid = (dist <= P) & (s_abs >= 0) & (s_abs < S)
        bias = np.where(valid[None], -slopes[:, None, None] * dist[None], np.float32(-1e30))
        table[t, :, :QH * 3 * P] = bias.transpose(1, 0, 2).reshape(P, -1)
        for g, w in enumerate(windows):
            at = t * P + np.arange(P)
            n = np.clip(at + w - w // 2, 0, S) - np.clip(at - w // 2, 0, S)
            table[t, :, QH * 3 * P + g] = np.float32(1.0) / n.astype(np.float32)
    band = np.zeros((P, 3, GROUPS, P), np.float32)
    s, t = np.arange(P)[:, None], np.arange(P)[None, :]
    for b in range(3):
        for g, w in enumerate(windows):
            d = s + (b - 1) * P - t
            band[:, b, g, :] = (d >= -(w // 2)) & (d < w - w // 2)
    return {"identity": np.eye(P, dtype=np.float32), "band": band,
            "bias_table": table.reshape(tiles * P, -1),
            "iota16": np.tile(np.arange(TOPK, dtype=np.float32), (P, 1))}


def kernel(**inputs):
    import numpy as np
    import concourse.bacc as bacc
    from concourse.bass_utils import run_bass_kernel_spmd

    a = {n: np.asarray(inputs[n]) for n in _INS}
    S, D = a["x"].shape[1:]
    lay = {
        "x": a["x"][0], "norm1_g": a["norm1_g"][0], "w_in": a["w_in"][0], "sink_logits": a["sink_logits"][0],
        "pool_w": a["pool_w"][0], "pool_scale": a["pool_scale"][0].reshape(GROUPS, P).T,
        "w_branch": a["w_branch"][0].reshape(-1, D), "w_gate": a["w_gate"][0], "b_gate": a["b_gate"][0],
        "w_out": a["w_out"][0], "norm2_g": a["norm2_g"][0], "w_query": a["peer_w_query"][0],
        "sub_keys_t": a["peer_sub_keys"][0].transpose(3, 0, 1, 2).reshape(P, PEER_HEADS * 2, N_KEYS),
        "peer_u": a["peer_u"][0], "peer_v": a["peer_v"][0], "norm_final_g": a["norm_final_g"],
    }
    lay.update(_constants(S))
    nc = bacc.Bacc("TRN2", target_bir_lowering=False, num_devices=1)
    arrays, args = {}, {}
    for name, value in lay.items():
        arrays[f"in_{name}"] = np.ascontiguousarray(value)
        args[name] = nc.dram_tensor(f"in_{name}", value.shape, mybir.dt.from_np(value.dtype), kind="ExternalInput").ap()
    out = nc.dram_tensor("out_0", (S, D), F32, kind="ExternalOutput").ap()
    encoder_block(nc, out=out, **args)
    r = run_bass_kernel_spmd(nc, [arrays], core_ids=[0])
    return r.results[0]["out_0"].reshape(1, S, D)
```

```python
from contextlib import ExitStack

import concourse.bass as bass
from concourse import mybir

F32 = mybir.dt.float32
U32 = mybir.dt.uint32
ALU = mybir.AluOpType
ACT = mybir.ActivationFunctionType
AX = mybir.AxisListType

P = 128
EPS = 1e-6
LOWEST = -3.4028234663852886e38
HEAD_DIM = 64
QH = 8
KVH = 2
GROUPS = 4
PEER_HEADS = 8
TOPK = 16
N_KEYS = 128
BANK = 512
RING = 8
ROUTE_STEPS = 32


class Steps:

    def __init__(self, sem, per):
        self.sem, self.per, self.base, self.n = sem, per, 0, 0

    def begin(self, t):
        self.base, self.n = t * self.per, 0

    def add(self, instruction):
        self.n += 1
        assert self.n <= self.per
        return instruction.then_inc(self.sem, 1)

    def wait(self, engine):
        engine.wait_ge(self.sem, self.base + self.n)


def settle(engine, passed):
    engine.sem_inc(passed, 1)


def after(engine, sem, value):
    if not (isinstance(value, int) and value <= 0):
        engine.wait_ge(sem, value)


def every_tile(engine, tiles, body):
    body(0)
    with engine.Fori(1, tiles) as t:
        body(t)


class Ring:

    def __init__(self, banks, full, free, per):
        assert per % len(banks) == 0
        self.banks, self.full, self.free, self.per = banks, full, free, per

    def open(self, engine):
        engine.sem_inc(self.free, len(self.banks))

    def bank(self, k):
        return self.banks[k % len(self.banks)]

    def claim(self, engine, t, k):
        engine.wait_ge(self.free, t * self.per + k + 1)
        return self.bank(k)

    def filled(self, engine, t, k):
        after(engine, self.full, t * self.per + k + 1)
        return self.bank(k)

    def emptied(self, engine, t, k):
        engine.wait_ge(self.free, t * self.per + k + 1 + len(self.banks))


def encoder_block(nc, x, norm1_g, w_in, sink_logits, pool_w, pool_scale, w_branch, w_gate, b_gate,
                  w_out, norm2_g, w_query, sub_keys_t, peer_u, peer_v, norm_final_g,
                  identity, band, bias_table, iota16, out):
    S, D = x.shape
    TILES = S // P
    KC = D // P
    ATT = QH * HEAD_DIM
    KVW = KVH * HEAD_DIM
    PW = D // 2
    AC = ATT // P
    CW = 3 * P
    BW = QH * CW + GROUPS
    SETS = PEER_HEADS * 2
    HK = PEER_HEADS * TOPK

    qT_d = nc.dram_tensor("qT_scratch", (S, ATT), F32, kind="Internal").ap()
    kT_d = nc.dram_tensor("kT_scratch", (S + 2 * P, P), F32, kind="Internal").ap()
    v_d = nc.dram_tensor("v_scratch", (S + 2 * P, KVW), F32, kind="Internal").ap()
    u_d = nc.dram_tensor("u_scratch", (S + 2 * P, PW), F32, kind="Internal").ap()
    gate_d = nc.dram_tensor("gate_scratch", (S, 2 * D), F32, kind="Internal").ap()
    x1_d = nc.dram_tensor("x1_scratch", (S, D), F32, kind="Internal").ap()
    h2_d = nc.dram_tensor("h2_scratch", (S, D), F32, kind="Internal").ap()
    h2T_d = nc.dram_tensor("h2T_scratch", (S, D), F32, kind="Internal").ap()

    def rows(t, n=1):
        return bass.ds(t * P, n * P)

    with ExitStack() as ctx:
        def sem(name):
            return ctx.enter_context(nc.semaphore(name))

        psum = [ctx.enter_context(nc.psum_tensor(f"bank{i}", [P, BANK], F32)) for i in range(8)]

        def keep(name, shape, dt=F32):
            return ctx.enter_context(nc.sbuf_tensor(name, shape, dt))

        ident = keep("ident", [P, P])
        gain = keep("gain", [P, D])
        small = keep("small", [P, 16])

        region1 = keep("region1", [P, 10240])
        chosen = region1[:, RING * D:RING * D + TILES * HK].bitcast(U32)
        weight = region1[:, RING * D + TILES * HK:RING * D + 2 * TILES * HK]
        region2 = keep("region2", [P, 16384])
        region3 = keep("region3", [P, 16384])

        def carve(region):
            at = [0]

            def take(n, dt=F32):
                at[0] += n
                assert at[0] <= region.shape[1], at
                return region[:, at[0] - n:at[0]] if dt is F32 else region[:, at[0] - n:at[0]].bitcast(dt)
            return take

        win_sb = region1[:, 0:KC * 1280].rearrange("p (k n) -> p k n", k=KC)
        wg_sb = region2[:, :].rearrange("p (k n) -> p k n", k=KC)
        wb_sb = region3[:, 0:2 * AC * D].rearrange("p (b k n) -> p b k n", b=2, k=AC)
        wo_sb = region3[:, 2 * AC * D:].rearrange("p (k n) -> p k n", k=KC)
        wq_sb = region2[:, :].rearrange("p (k n) -> p k n", k=KC)

        const_in = sem("const_in")
        IN_PARTS = ((0, ATT), (ATT, 2 * KVW), (ATT + 2 * KVW, PW))
        GCH = 2 * D // BANK
        win_in = [sem(f"win_in{i}") for i in range(len(IN_PARTS))]
        wg_in = [sem(f"wg_in{c}") for c in range(GCH)]
        bg_in = sem("b_gate_in")
        wbo_in = sem("wbo_in")
        wq_in = sem("wq_in")
        eps_ready = sem("eps_ready")
        passed = sem("waits_passed")

        with ExitStack() as pctx:
            def tmp(name, shape, dt=F32):
                return pctx.enter_context(nc.sbuf_tensor(name, shape, dt))
            xin = tmp("xin", [P, D])
            h = tmp("h", [P, D])
            hT = tmp("hT", [P, KC, P])
            gates = region3[:, 0:2 * D]
            bg = region3[:, 2 * D:4 * D]
            zeros = region3[:, 4 * D:4 * D + PW]
            q_sb = tmp("q_sb", [P, ATT])
            k_sb = tmp("k_sb", [P, P])
            v_sb = tmp("v_sb", [P, KVW])
            u_sb = tmp("u_sb", [P, PW])
            qT = tmp("qT_out", [P, ATT])
            kT = tmp("kT_out", [P, P])
            x_in = sem("x_in")
            sumsq_ready = sem("sumsq_ready")
            rms_ready = sem("rms_ready")
            rstd_ready = sem("rstd_ready")
            h_ready = sem("h_ready")
            by_act = Ring(psum[0:2], sem("project_act_full"), sem("project_act_free"), 6)
            by_dve = Ring(psum[2:7], sem("project_dve_full"), sem("project_dve_free"), 5)
            v_ready = sem("v_ready")
            gate_ready = sem("gate_ready")
            zero_ready = sem("zero_ready")
            pads_out = sem("pads_out")
            qT_out, kT_out, v_out, u_out, g_out = (
                sem(n) for n in ("qT_stored", "kT_stored", "v_stored", "u_stored", "gates_stored"))
            HT, Q, KV, QT, KT = 0, 2, 3, 4, 5
            U, G = 0, 1

            with nc.Block() as block:
                @block.sync
                def _(sp):
                    sp.dma_start(xin[:, :], x[0:P, :]).then_inc(x_in, 16)
                    sp.dma_start(ident[:, :], identity).then_inc(const_in, 16)
                    sp.dma_start(gain[:, :], norm1_g.partition_broadcast(P)).then_inc(const_in, 16)
                    for use, (at, n) in enumerate(IN_PARTS):
                        sp.dma_start(win_sb[:, :, at:at + n], w_in[:, at:at + n].rearrange("(k p) n -> p k n", p=P)
                                     ).then_inc(win_in[use], 16)
                    sp.dma_start(bg, b_gate.partition_broadcast(P)).then_inc(bg_in, 16)
                    for c in range(GCH):
                        part = slice(c * BANK, (c + 1) * BANK)
                        sp.dma_start(wg_sb[:, :, part], w_gate[:, part].rearrange("(k p) n -> p k n", p=P)
                                     ).then_inc(wg_in[c], 16)
                    with sp.Fori(1, TILES) as t:
                        sp.wait_ge(h_ready, t)
                        sp.dma_start(xin[:, :], x[rows(t), :]).then_inc(x_in, 16)
                    sp.dma_start(wo_sb, w_out.rearrange("(k p) n -> p k n", p=P)).then_inc(wbo_in, 16)
                    sp.wait_ge(pads_out, 6 * 16)
                    for b in (1, 0):
                        if b == 0:
                            sp.wait_ge(g_out, 16 * TILES)
                        sp.dma_start(wb_sb[:, b, :, :], w_branch[b * ATT:(b + 1) * ATT, :].rearrange(
                            "(k p) n -> p k n", p=P)).then_inc(wbo_in, 16)

                @block.gpsimd
                def _(pool):
                    nc.gpsimd.memset(zeros, 0.0).then_inc(zero_ready, 1)
                    pool.wait_ge(zero_ready, 1)
                    for at in (0, S + P):
                        pool.dma_start(kT_d[at:at + P, :], zeros[:, 0:P]).then_inc(pads_out, 16)
                        pool.dma_start(v_d[at:at + P, :], zeros[:, 0:KVW]).then_inc(pads_out, 16)
                        pool.dma_start(u_d[at:at + P, :], zeros).then_inc(pads_out, 16)
                    with pool.Fori(0, TILES) as t:
                        pool.wait_ge(v_ready, t + 1)
                        settle(pool, passed)
                        pool.dma_start(v_d[rows(t + 1), :], v_sb[:, :]).then_inc(v_out, 16)
                        by_dve.emptied(pool, t, U)
                        settle(pool, passed)
                        pool.dma_start(u_d[rows(t + 1), :], u_sb[:, :]).then_inc(u_out, 16)
                        by_act.emptied(pool, t, QT)
                        settle(pool, passed)
                        pool.dma_start(qT_d[rows(t), :], qT[:, :]).then_inc(qT_out, 16)
                        by_act.emptied(pool, t, KT)
                        settle(pool, passed)
                        pool.dma_start(kT_d[rows(t + 1), :], kT[:, :]).then_inc(kT_out, 16)
                        pool.wait_ge(gate_ready, t + 1)
                        settle(pool, passed)
                        pool.dma_start(gate_d[rows(t), :], gates).then_inc(g_out, 16)
                    pool.wait_ge(pads_out, 6 * 16)
                    for stored in (qT_out, kT_out, v_out, u_out, g_out):
                        pool.wait_ge(stored, 16 * TILES)

                @block.scalar
                def _(act):
                    by_act.open(act)
                    act.wait_ge(eps_ready, 1)
                    def body(t):
                        act.wait_ge(x_in, 16 * t + 16)
                        after(act, rstd_ready, t)
                        nc.scalar.activation(h[:, :], xin[:, :], ACT.Square, accum_out=small[:, 0:1]
                                             ).then_inc(sumsq_ready, 1)
                        act.wait_ge(sumsq_ready, t + 1)
                        nc.scalar.activation(small[:, 1:2], small[:, 0:1], ACT.Sqrt, bias=small[:, 14:15],
                                             scale=1.0 / D).then_inc(rms_ready, 1)
                        by_dve.filled(act, t, -1)
                        for half in range(2):
                            bank = by_act.filled(act, t, HT + half)
                            nc.scalar.activation(hT[:, 4 * half:4 * half + 4, :],
                                                 bank[:, :].rearrange("p (k n) -> p k n", k=4),
                                                 ACT.Copy).then_inc(by_act.free, 1)
                        bank = by_act.filled(act, t, Q)
                        nc.scalar.activation(q_sb[:, :].rearrange("p (c g d) -> p g c d", c=4, g=KVH),
                                             bank[:, :].rearrange("p (g c d) -> p g c d", g=KVH, c=4),
                                             ACT.Copy).then_inc(by_act.free, 1)
                        bank = by_act.filled(act, t, KV)
                        after(act, v_out, 16 * t)
                        nc.scalar.activation(v_sb[:, :], bank[:, P:P + KVW], ACT.Copy).then_inc(v_ready, 1)
                        nc.scalar.activation(k_sb[:, :], bank[:, 0:P], ACT.Copy).then_inc(by_act.free, 1)
                        bank = by_act.filled(act, t, QT)
                        after(act, qT_out, 16 * t)
                        nc.scalar.activation(qT[:, :], bank[:, :], ACT.Copy).then_inc(by_act.free, 1)
                        bank = by_act.filled(act, t, KT)
                        after(act, kT_out, 16 * t)
                        nc.scalar.activation(kT[:, :], bank[:, 0:P], ACT.Copy).then_inc(by_act.free, 1)
                        by_dve.emptied(act, t, G + GCH - 1)
                        nc.scalar.activation(gates, gates, ACT.Sigmoid).then_inc(gate_ready, 1)

                    every_tile(act, TILES, body)

                @block.vector
                def _(dve):
                    by_dve.open(dve)
                    nc.vector.memset(small[:, 14:15], EPS).then_inc(eps_ready, 1)
                    dve.wait_ge(const_in, 32)
                    def body(t):
                        dve.wait_ge(rms_ready, t + 1)
                        nc.vector.reciprocal(small[:, 2:3], small[:, 1:2]).then_inc(rstd_ready, 1)
                        dve.wait_ge(rstd_ready, t + 1)
                        nc.vector.scalar_tensor_tensor(out=h[:, :], in0=xin[:, :], scalar=small[:, 2:3],
                                                       in1=gain[:, :], op0=ALU.mult, op1=ALU.mult
                                                       ).then_inc(h_ready, 1)
                        bank = by_dve.filled(dve, t, U)
                        after(dve, u_out, 16 * t)
                        nc.vector.tensor_copy(u_sb[:, :], bank[:, :]).then_inc(by_dve.free, 1)
                        after(dve, g_out, 16 * t)
                        dve.wait_ge(bg_in, 16)
                        for c in range(GCH):
                            bank = by_dve.filled(dve, t, G + c)
                            part = slice(c * BANK, (c + 1) * BANK)
                            nc.vector.tensor_tensor(gates[:, part], bank[:, :], bg[:, part], ALU.add
                                                    ).then_inc(by_dve.free, 1)

                    every_tile(dve, TILES, body)

                @block.tensor
                def _(pe):
                    def project(t, ring, use, w, n):
                        bank = ring.claim(pe, t, use)
                        for k in range(KC):
                            last = nc.tensor.matmul(bank[:, 0:n], hT[:, k, :], w[:, k, :],
                                                    start=(k == 0), stop=(k == KC - 1))
                        last.then_inc(ring.full, 1)

                    pe.wait_ge(const_in, 32)
                    with pe.Fori(0, TILES) as t:
                        pe.wait_ge(h_ready, t + 1)
                        for half in range(2):
                            bank = by_act.claim(pe, t, HT + half)
                            for k in range(4):
                                c = (4 * half + k) * P
                                last = nc.tensor.transpose(bank[:, k * P:(k + 1) * P], h[:, c:c + P], ident[:, :])
                            last.then_inc(by_act.full, 1)
                        by_act.emptied(pe, t, HT + 1)
                        for (ring, use), arrived, (at, n) in zip(((by_act, Q), (by_act, KV), (by_dve, U)),
                                                                 win_in, IN_PARTS):
                            pe.wait_ge(arrived, 16)
                            project(t, ring, use, win_sb[:, :, at:at + n], n)
                        bank = by_act.claim(pe, t, QT)
                        for c in range(AC):
                            last = nc.tensor.transpose(bank[:, c * P:(c + 1) * P], q_sb[:, c * P:(c + 1) * P],
                                                       ident[:, :])
                        last.then_inc(by_act.full, 1)
                        bank = by_act.claim(pe, t, KT)
                        nc.tensor.transpose(bank[:, 0:P], k_sb[:, :], ident[:, :]).then_inc(by_act.full, 1)
                        for c in range(GCH):
                            pe.wait_ge(wg_in[c], 16)
                            project(t, by_dve, G + c, wg_sb[:, :, c * BANK:(c + 1) * BANK], BANK)

        with ExitStack() as mctx:
            def tmp(name, shape, dt=F32):
                return mctx.enter_context(nc.sbuf_tensor(name, shape, dt))
            take = carve(region1)
            bias = take(BW)
            L = bias[:, 0:QH * CW].rearrange("p (h c) -> p h c", h=QH)
            rcount = bias[:, QH * CW:BW]
            qT = take(ATT).rearrange("p (c n) -> p c n", c=4)
            kw = take(CW).rearrange("p (b n) -> p b n", b=3)
            vw = take(3 * KVW).rearrange("p (b n) -> p b n", b=3)
            uw = take(3 * PW).rearrange("p (b n) -> p b n", b=3)
            PT = take(2 * CW).rearrange("p (s b n) -> p s b n", s=2, b=3)
            o_sb = take(ATT)
            oT = take(ATT).rearrange("p (k n) -> p k n", k=AC)
            mixed = take(PW)
            mixedT = take(PW).rearrange("p (g n) -> p g n", g=GROUPS)
            opT = take(PW).rearrange("p (k n) -> p k n", k=AC)
            gates = tmp("gates_in", [P, 2 * D])
            xres = tmp("xres", [P, D])
            h2 = tmp("h2_new", [P, D])[:, :]
            mT = tmp("mT", [P, KC, P])
            x1 = tmp("x1", [P, D])
            h2T = tmp("h2T_out", [P, D])
            band_sb = tmp("band_sb", [P, 3, GROUPS, P])
            pw_sb = take(GROUPS * P).rearrange("p (g n) -> p g n", g=GROUPS)
            ps_sb = tmp("ps_sb", [P, GROUPS])
            sink = tmp("sink", [P, QH])
            nsink = tmp("nsink", [P, QH])
            nmax = tmp("nmax", [P, QH])
            nshift = tmp("nshift", [P, QH])
            sdiff = tmp("sdiff", [P, QH])
            sexp = tmp("sexp", [P, QH])
            rsum = tmp("rsum", [P, QH])
            den = tmp("den", [P, QH])
            rden = tmp("rden", [P, QH])
            mconst_in, nsink_ready = sem("mix_const_in"), sem("nsink_ready")
            bias_in, qk_in, vu_in, gx_in = sem("bias_in"), sem("qk_in"), sem("vu_in"), sem("gx_in")
            shift_ready, exp_ready = sem("shift_ready"), sem("exp_ready")
            rden_ready, pv_done = sem("rden_ready"), sem("pv_done")
            softmax = Steps(sem("softmax_steps"), 4)
            merged_ready = sem("merged_ready")
            sumsq_ready, rms_ready, rstd_ready, h2_ready = (
                sem(n) for n in ("sumsq1_ready", "rms1_ready", "rstd1_ready", "h2_ready"))
            x1_out, h2_out, h2T_out = sem("x1_stored"), sem("h2_stored"), sem("h2T_stored")
            a_dve = Ring(psum[0:2], sem("a_dve_full"), sem("a_dve_free"), 12)
            a_act = Ring(psum[2:4], sem("a_act_full"), sem("a_act_free"), 10)
            b_dve = Ring(psum[4:6], sem("b_dve_full"), sem("b_dve_free"), 6)
            b_act = Ring(psum[6:8], sem("b_act_full"), sem("b_act_free"), 4)
            LOGITS, POOLED, ATTN, MIXED = 0, 8, 9, 10
            PTR, OT, MIXEDT = 0, 8, 9
            BRANCH, OUT = 0, 4
            MT, H2T = 0, 2
            EXPS = QH + 1

            def pipeline(engine, attend, norm, branch, weigh, output, finish):
                def stages(t, now=True, before=True, two_before=True):
                    if now:
                        attend(t)
                    if two_before:
                        norm(t - 2)
                    if before:
                        branch(t - 1)
                    if now:
                        weigh(t)
                    if before:
                        output(t - 1)
                    if now:
                        finish(t)

                for t in range(3):
                    stages(t, before=t > 0, two_before=t > 1)
                with engine.Fori(3, TILES) as t:
                    stages(t)
                stages(TILES, now=False)
                norm(TILES - 1)

            with nc.Block() as block:
                @block.sync
                def _(sp):
                    sp.dma_start(gain[:, :], norm2_g.partition_broadcast(P)).then_inc(mconst_in, 16)

                    def attend(t, first=False):
                        if not first:
                            a_act.filled(sp, t - 1, PTR + QH - 1)
                            a_dve.emptied(sp, t - 1, POOLED)
                        sp.dma_start(bias, bias_table[rows(t), :]).then_inc(bias_in, 16)
                        sp.dma_start(qT, qT_d[rows(t), :].rearrange("p (c n) -> p c n", c=4)).then_inc(qk_in, 16)
                        sp.dma_start(kw, kT_d[rows(t, 3), :].rearrange("(b p) n -> p b n", p=P)).then_inc(qk_in, 16)
                        if not first:
                            a_dve.filled(sp, t - 1, ATTN)
                        sp.dma_start(vw, v_d[rows(t, 3), :].rearrange("(b p) n -> p b n", p=P)).then_inc(vu_in, 16)
                        sp.dma_start(uw, u_d[rows(t, 3), :].rearrange("(b p) n -> p b n", p=P)).then_inc(vu_in, 16)

                    def merge(t, first=False):
                        if not first:
                            b_dve.emptied(sp, t - 1, OUT + 1)
                            b_act.filled(sp, t - 1, MT + 1)
                        sp.dma_start(gates[:, :], gate_d[rows(t), :]).then_inc(gx_in, 16)
                        sp.dma_start(xres[:, :], x[rows(t), :]).then_inc(gx_in, 16)

                    attend(0, True)
                    merge(0, True)
                    sp.dma_start(band_sb[:, :, :, :], band).then_inc(mconst_in, 16)
                    sp.dma_start(pw_sb, pool_w.rearrange("g c d -> c g d")).then_inc(mconst_in, 16)
                    sp.dma_start(ps_sb[:, :], pool_scale).then_inc(mconst_in, 16)
                    sp.dma_start(sink[:, :], sink_logits.partition_broadcast(P)).then_inc(mconst_in, 16)
                    sp.dma_start(wq_sb, w_query.rearrange("(k p) n -> p k n", p=P)).then_inc(wq_in, 16)
                    with sp.Fori(1, TILES) as t:
                        attend(t)
                        merge(t)

                @block.gpsimd
                def _(pool):
                    with pool.Fori(0, TILES) as t:
                        b_dve.emptied(pool, t, OUT + 1)
                        settle(pool, passed)
                        pool.dma_start(x1_d[rows(t), :], x1[:, :]).then_inc(x1_out, 16)
                        pool.wait_ge(h2_ready, t + 1)
                        settle(pool, passed)
                        pool.dma_start(h2_d[rows(t), :], h2).then_inc(h2_out, 16)
                        b_act.emptied(pool, t, H2T + 1)
                        settle(pool, passed)
                        pool.dma_start(h2T_d[rows(t), :], h2T[:, :]).then_inc(h2T_out, 16)
                    for stored in (x1_out, h2_out, h2T_out):
                        pool.wait_ge(stored, 16 * TILES)

                @block.tensor
                def _(pe):
                    def attend(t):
                        pe.wait_ge(qk_in, 32 * t + 32)
                        for hd in range(QH):
                            g, c = divmod(hd, 4)
                            half = slice(g * HEAD_DIM, (g + 1) * HEAD_DIM)
                            bank = a_dve.claim(pe, t, LOGITS + hd)
                            nc.tensor.matmul(bank[:, 0:CW], qT[half, c, :],
                                             kw[half, :, :].rearrange("p b n -> p (b n)"), start=True, stop=True
                                             ).then_inc(a_dve.full, 1)
                        pe.wait_ge(vu_in, 32 * t + 32)
                        bank = a_dve.claim(pe, t, POOLED)
                        for g in range(GROUPS):
                            for b in range(3):
                                last = nc.tensor.matmul(bank[:, g * P:(g + 1) * P], band_sb[:, b, g, :],
                                                        uw[:, b, g * P:(g + 1) * P], start=(b == 0), stop=(b == 2))
                        last.then_inc(a_dve.full, 1)

                    def weigh(t):
                        def weigh_head(hd):
                            a_act.emptied(pe, t, PTR + hd)
                            g = hd // 4
                            for b in range(3):
                                last = nc.tensor.matmul(a_dve.bank(ATTN)[:, hd * HEAD_DIM:(hd + 1) * HEAD_DIM],
                                                        PT[:, hd % 2, b, :],
                                                        vw[:, b, g * HEAD_DIM:(g + 1) * HEAD_DIM],
                                                        start=(b == 0), stop=(b == 2))
                            last.then_inc(pv_done if hd < QH - 1 else a_dve.full, 1)

                        a_dve.claim(pe, t, ATTN)
                        for hd in range(QH):
                            pe.wait_ge(exp_ready, EXPS * t + hd + 1)
                            bank = a_act.claim(pe, t, PTR + hd)
                            for b in range(3):
                                last = nc.tensor.transpose(bank[:, b * P:(b + 1) * P], L[:, hd, b * P:(b + 1) * P],
                                                           ident[:, :])
                            last.then_inc(a_act.full, 1)
                            if hd:
                                weigh_head(hd - 1)
                        weigh_head(QH - 1)

                    def finish(t):
                        a_dve.emptied(pe, t, POOLED)
                        a_dve.emptied(pe, t, ATTN)
                        for use, rows_of in ((OT, o_sb), (MIXEDT, mixed)):
                            bank = a_act.claim(pe, t, use)
                            for c in range(AC):
                                last = nc.tensor.transpose(bank[:, c * P:(c + 1) * P], rows_of[:, c * P:(c + 1) * P],
                                                           ident[:, :])
                            last.then_inc(a_act.full, 1)
                        a_act.emptied(pe, t, MIXEDT)
                        for two in range(2):
                            bank = a_dve.claim(pe, t, MIXED + two)
                            for i in range(2):
                                g = 2 * two + i
                                last = nc.tensor.matmul(bank[:, i * P:(i + 1) * P], pw_sb[:, g, :], mixedT[:, g, :],
                                                        start=True, stop=True)
                            last.then_inc(a_dve.full, 1)

                    def branch(t):
                        a_act.emptied(pe, t, OT)
                        a_dve.emptied(pe, t, MIXED + 1)
                        for c in range(2):
                            for b, of in enumerate((oT, opT)):
                                bank = b_dve.claim(pe, t, BRANCH + 2 * c + b)
                                for k in range(AC):
                                    last = nc.tensor.matmul(bank[:, :], of[:, k, :],
                                                            wb_sb[:, b, k, c * BANK:(c + 1) * BANK],
                                                            start=(k == 0), stop=(k == AC - 1))
                                last.then_inc(b_dve.full, 1)

                    def output(t):
                        for c in range(2):
                            pe.wait_ge(merged_ready, 2 * t + c + 1)
                            bank = b_act.claim(pe, t, MT + c)
                            for k in range(4):
                                at = c * BANK + k * P
                                last = nc.tensor.transpose(bank[:, k * P:(k + 1) * P], gates[:, at:at + P], ident[:, :])
                            last.then_inc(b_act.full, 1)
                        b_act.emptied(pe, t, MT + 1)
                        for c in range(2):
                            bank = b_dve.claim(pe, t, OUT + c)
                            for k in range(KC):
                                last = nc.tensor.matmul(bank[:, :], mT[:, k, :], wo_sb[:, k, c * BANK:(c + 1) * BANK],
                                                        start=(k == 0), stop=(k == KC - 1))
                            last.then_inc(b_dve.full, 1)

                    def norm(t):
                        pe.wait_ge(h2_ready, t + 1)
                        for c in range(2):
                            bank = b_act.claim(pe, t, H2T + c)
                            for k in range(4):
                                at = c * BANK + k * P
                                last = nc.tensor.transpose(bank[:, k * P:(k + 1) * P], h2[:, at:at + P], ident[:, :])
                            last.then_inc(b_act.full, 1)

                    pe.wait_ge(mconst_in, 80)
                    pe.wait_ge(wbo_in, 48)
                    pipeline(pe, attend, norm, branch, weigh, output, finish)

                @block.scalar
                def _(act):
                    def attend(t):
                        act.wait_ge(shift_ready, 2 * t + 2)
                        for hd in range(QH):
                            nc.scalar.activation(L[:, hd, :], L[:, hd, :], ACT.Exp, bias=nshift[:, hd:hd + 1],
                                                 accum_out=rsum[:, hd:hd + 1]).then_inc(exp_ready, 1)
                        nc.scalar.activation(sexp[:, :], sdiff[:, :], ACT.Exp).then_inc(exp_ready, 1)

                    def weigh(t):
                        for hd in range(QH):
                            bank = a_act.filled(act, t, PTR + hd)
                            if hd >= 2:
                                act.wait_ge(pv_done, (QH - 1) * t + hd - 1)
                            nc.scalar.activation(PT[:, hd % 2, :, :], bank[:, 0:CW].rearrange("p (b n) -> p b n", b=3),
                                                 ACT.Copy).then_inc(a_act.free, 1)

                    def finish(t):
                        for use, to in ((OT, oT), (MIXEDT, mixedT)):
                            bank = a_act.filled(act, t, use)
                            nc.scalar.activation(to, bank[:, :].rearrange("p (k n) -> p k n", k=AC),
                                                 ACT.Copy).then_inc(a_act.free, 1)

                    def branch(t):
                        pass

                    def output(t):
                        for c in range(2):
                            bank = b_act.filled(act, t, MT + c)
                            nc.scalar.activation(mT[:, 4 * c:4 * c + 4, :], bank[:, :].rearrange("p (k n) -> p k n", k=4),
                                                 ACT.Copy).then_inc(b_act.free, 1)
                        b_dve.emptied(act, t, OUT + 1)
                        after(act, h2_out, 16 * t)
                        nc.scalar.activation(h2, x1[:, :], ACT.Square, accum_out=small[:, 0:1]).then_inc(sumsq_ready, 1)
                        act.wait_ge(sumsq_ready, t + 1)
                        nc.scalar.activation(small[:, 1:2], small[:, 0:1], ACT.Sqrt, bias=small[:, 14:15],
                                             scale=1.0 / D).then_inc(rms_ready, 1)

                    def norm(t):
                        for c in range(2):
                            bank = b_act.filled(act, t, H2T + c)
                            if c == 0:
                                after(act, h2T_out, 16 * t)
                            nc.scalar.activation(h2T[:, c * BANK:(c + 1) * BANK], bank[:, :], ACT.Copy
                                                 ).then_inc(b_act.free, 1)

                    a_act.open(act)
                    b_act.open(act)
                    pipeline(act, attend, norm, branch, weigh, output, finish)

                @block.vector
                def _(dve):
                    def attend(t):
                        softmax.begin(t)
                        dve.wait_ge(bias_in, 16 * t + 16)
                        for hd in range(QH):
                            bank = a_dve.filled(dve, t, LOGITS + hd)
                            nc.vector.scalar_tensor_tensor(out=L[:, hd, :], in0=bank[:, 0:CW], scalar=HEAD_DIM ** -0.5,
                                                           in1=L[:, hd, :], op0=ALU.mult, op1=ALU.add
                                                           ).then_inc(a_dve.free, 1)
                        a_dve.emptied(dve, t, LOGITS + QH - 1)
                        softmax.add(nc.vector.reduce_max(nmax[:, :], L, AX.X, negate=True))
                        softmax.wait(dve)
                        nc.vector.tensor_tensor(nshift[:, :], nmax[:, :], nsink[:, :], ALU.min).then_inc(shift_ready, 1)
                        dve.wait_ge(shift_ready, 2 * t + 1)
                        nc.vector.tensor_tensor(sdiff[:, :], sink[:, :], nshift[:, :], ALU.add).then_inc(shift_ready, 1)
                        bank = a_dve.filled(dve, t, POOLED)
                        for g in range(GROUPS):
                            part = slice(g * P, (g + 1) * P)
                            last = nc.vector.scalar_tensor_tensor(out=mixed[:, part], in0=bank[:, part],
                                                                  scalar=rcount[:, g:g + 1], in1=uw[:, 1, part],
                                                                  op0=ALU.mult, op1=ALU.subtract)
                        last.then_inc(a_dve.free, 1)

                    def weigh(t):
                        dve.wait_ge(exp_ready, EXPS * (t + 1))
                        softmax.add(nc.vector.tensor_tensor(den[:, :], rsum[:, :], sexp[:, :], ALU.add))
                        softmax.wait(dve)
                        softmax.add(nc.vector.reciprocal(rden[:, :], den[:, :]))
                        softmax.wait(dve)
                        bank = a_dve.filled(dve, t, ATTN)
                        nc.vector.tensor_tensor(o_sb.rearrange("p (h d) -> p h d", h=QH),
                                                bank[:, :].rearrange("p (h d) -> p h d", h=QH),
                                                rden[:, :].unsqueeze(2).to_broadcast([P, QH, HEAD_DIM]), ALU.mult
                                                ).then_inc(a_dve.free, 1)
                        softmax.add(nc.vector.memset(small[:, 13:14], 0.0))

                    def finish(t):
                        for two in range(2):
                            bank = a_dve.filled(dve, t, MIXED + two)
                            nc.vector.tensor_tensor(opT[:, 2 * two:2 * two + 2, :],
                                                    bank[:, 0:2 * P].rearrange("p (g n) -> p g n", g=2),
                                                    ps_sb[:, 2 * two:2 * two + 2].unsqueeze(2).to_broadcast([P, 2, P]),
                                                    ALU.mult).then_inc(a_dve.free, 1)

                    def branch(t):
                        dve.wait_ge(gx_in, 32 * t + 32)
                        for c in range(2):
                            for b in range(2):
                                bank = b_dve.filled(dve, t, BRANCH + 2 * c + b)
                                part = gates[:, b * D + c * BANK:b * D + (c + 1) * BANK]
                                nc.vector.tensor_tensor(part, bank[:, :], part, ALU.mult).then_inc(b_dve.free, 1)
                            b_dve.emptied(dve, t, BRANCH + 2 * c + 1)
                            to = gates[:, c * BANK:(c + 1) * BANK]
                            nc.vector.tensor_tensor(to, to, gates[:, D + c * BANK:D + (c + 1) * BANK], ALU.add
                                                    ).then_inc(merged_ready, 1)

                    def output(t):
                        after(dve, x1_out, 16 * t)
                        for c in range(2):
                            bank = b_dve.filled(dve, t, OUT + c)
                            part = slice(c * BANK, (c + 1) * BANK)
                            nc.vector.tensor_tensor(x1[:, part], bank[:, :], xres[:, part], ALU.add
                                                    ).then_inc(b_dve.free, 1)
                        dve.wait_ge(rms_ready, t + 1)
                        nc.vector.reciprocal(small[:, 2:3], small[:, 1:2]).then_inc(rstd_ready, 1)
                        dve.wait_ge(rstd_ready, t + 1)
                        nc.vector.scalar_tensor_tensor(out=h2, in0=x1[:, :], scalar=small[:, 2:3], in1=gain[:, :],
                                                       op0=ALU.mult, op1=ALU.mult).then_inc(h2_ready, 1)

                    def norm(t):
                        pass

                    a_dve.open(dve)
                    b_dve.open(dve)
                    dve.wait_ge(mconst_in, 80)
                    nc.vector.tensor_scalar(nsink[:, :], sink[:, :], -1.0, None, ALU.mult).then_inc(nsink_ready, 1)
                    dve.wait_ge(nsink_ready, 1)
                    pipeline(dve, attend, norm, branch, weigh, output, finish)

        def tmp(name, shape, dt=F32):
            return ctx.enter_context(nc.sbuf_tensor(name, shape, dt))
        take = carve(region1)
        u_rows = take(RING * D).rearrange("p (s n) -> p s n", s=RING)
        take = carve(region3)
        v_rows = take(RING * D).rearrange("p (s n) -> p s n", s=RING)
        h2_next, h2_now, x1_now, x2, y = (take(D) for _ in range(5))
        sk_sb = take(SETS * N_KEYS).rearrange("p (s n) -> p s n", s=SETS)
        CS = BANK // P
        CHUNKS = SETS // CS
        q_sb = take(BANK)
        qT = take(BANK).rearrange("p (s n) -> p s n", s=CS)
        scores = tmp("scores", [P, CS, N_KEYS])
        cand = tmp("cand", [P, PEER_HEADS * TOPK * TOPK])
        cand3 = cand[:, :].rearrange("p (h n) -> p h n", h=PEER_HEADS)
        cand4 = cand[:, :].rearrange("p (h a b) -> p h a b", h=PEER_HEADS, a=TOPK)
        hit = tmp("hit", [P, HK * TOPK])
        hit4 = hit[:, :].rearrange("p (h k a) -> p h k a", h=PEER_HEADS, k=TOPK)
        hit3 = hit[:, :].rearrange("p (n a) -> p n a", a=TOPK)
        top = tmp("top", [P, SETS, TOPK])
        topi = tmp("topi", [P, SETS, TOPK], U32)
        topf = tmp("topf", [P, SETS, TOPK])
        best = tmp("best", [P, PEER_HEADS, TOPK])
        pos = tmp("pos", [P, PEER_HEADS, TOPK], U32)
        half_pos = tmp("half_pos", [P, 2, HK], U32)
        half_f = tmp("half_f", [P, 2, PEER_HEADS, TOPK])
        found = tmp("found", [P, 2, HK])
        shifted = tmp("shifted", [P, HK])
        wsum = tmp("wsum", [P, PEER_HEADS])
        rwsum = tmp("rwsum", [P, PEER_HEADS])
        iota_sb = tmp("iota_sb", [P, TOPK])
        h2T = tmp("h2T_in", [P, D])
        DIAGS = 4
        diag = tmp("diag", [P, DIAGS, P])
        dots = tmp("dots", [P, 2, TOPK])
        gelu = tmp("gelu", [P, 2, TOPK])
        coef = tmp("coef", [P, 2, TOPK])
        rowid = tmp("rowid", [P, 2, TOPK], U32)

        rconst_in, h2T_in = sem("route_const_in"), sem("h2T_loaded")
        scores_used = sem("scores_used")
        shifted_ready, wexp_ready = sem("shifted_ready"), sem("wexp_ready")
        chosen_ready, weight_ready = sem("chosen_ready"), sem("weight_ready")
        ring = Ring(psum[2:6], sem("route_full"), sem("route_free"), 3 * CHUNKS)
        QUERY, QUERYT, SCORE = range(3)
        topk = Steps(sem("topk_steps"), ROUTE_STEPS)
        u_in = [sem(f"u_rows_in{i}") for i in range(RING)]
        v_in = [sem(f"v_rows_in{i}") for i in range(RING)]
        u_used, v_used = sem("u_rows_used"), sem("v_rows_used")
        ids_ready, gelu_ready, coef_ready, diag_ready = (
            sem(n) for n in ("ids_ready", "gelu_ready", "coef_ready", "diag_ready"))
        h2n_in, x1n_in, h2_copied = sem("h2_next_in"), sem("x1_now_in"), sem("h2_copied")
        egain_in = sem("final_gain_in")
        x2_ready = sem("x2_ready")
        sumsq_ready, rms_ready = sem("sumsq2_ready"), sem("rms2_ready")
        rstd_ready = sem("rstd2_ready")
        y_ready, y_out, y_free = sem("y_ready"), sem("y_stored"), sem("y_free")
        acc = psum[0:2]

        def experts_with_route(engine, start, step, end, route_slice):
            for c in range(PEER_HEADS):
                route_slice(0, c)
            with engine.Fori(1, TILES) as t:
                start(t - 1)
                for hd in range(PEER_HEADS):
                    step(t - 1, (t - 1) * PEER_HEADS + hd, hd % 2, lambda: route_slice(t, hd), hd == 0)
                end(t - 1)
            start(TILES - 1)
            for hd in range(2):
                step(TILES - 1, (TILES - 1) * PEER_HEADS + hd, hd, lambda: None, hd == 0)
            with engine.Fori(1, PEER_HEADS // 2) as pair:
                for s in range(2):
                    step(TILES - 1, (TILES - 1) * PEER_HEADS + pair * 2 + s, s, lambda: None, False)
            end(TILES - 1)

        def nothing(*_):
            pass

        with nc.Block() as block:
            @block.sync
            def _(sp):
                sp.dma_start(h2T[:, :], h2T_d[0:P, :]).then_inc(h2T_in, 16)
                sp.dma_start(sk_sb, sub_keys_t).then_inc(rconst_in, 16)
                sp.dma_start(iota_sb[:, :], iota16).then_inc(rconst_in, 16)
                sp.dma_start(gain[:, :], norm_final_g.partition_broadcast(P)).then_inc(egain_in, 16)
                sp.dma_start(h2_next, h2_d[0:P, :]).then_inc(h2n_in, 16)
                sp.dma_start(x1_now, x1_d[0:P, :]).then_inc(x1n_in, 16)
                ring.filled(sp, 0, 3 * (CHUNKS - 1) + QUERY)
                sp.dma_start(h2T[:, :], h2T_d[P:2 * P, :]).then_inc(h2T_in, 16)

                def tile(t, another):
                    sp.wait_ge(h2_copied, t)
                    sp.dma_start(h2_next, h2_d[rows(t), :]).then_inc(h2n_in, 16)
                    if another:
                        ring.filled(sp, t, 3 * (CHUNKS - 1) + QUERY)
                        sp.dma_start(h2T[:, :], h2T_d[rows(t + 1), :]).then_inc(h2T_in, 16)
                    sp.wait_ge(x2_ready, 2 * t + 2)
                    sp.dma_start(x1_now, x1_d[rows(t), :]).then_inc(x1n_in, 16)
                    sp.wait_ge(y_ready, t)
                    sp.dma_start(out[rows(t - 1), :], y).then_inc(y_out, 16)
                    sp.wait_ge(y_out, 16 * t)
                    sp.sem_inc(y_free, 1)

                with sp.Fori(1, TILES - 1) as t:
                    tile(t, True)
                tile(TILES - 1, False)
                sp.wait_ge(y_ready, TILES)
                sp.dma_start(out[S - P:S, :], y).then_inc(y_out, 16)
                sp.wait_ge(y_out, 16 * TILES)

            @block.gpsimd
            def _(pool):
                def step(t, g, s):
                    nc.gpsimd.tensor_copy(rowid[:, s, :], chosen[:, bass.ds(g * TOPK, TOPK)]).then_inc(ids_ready, 1)
                    pool.wait_ge(ids_ready, g + 1)
                    for table, ring_rows, arrived, used in ((peer_u, u_rows, u_in, u_used), (peer_v, v_rows, v_in, v_used)):
                        for j in range(TOPK):
                            slot = j % RING
                            pool.wait_ge(used, g * TOPK + j + 1)
                            settle(pool, passed)
                            pool.indirect_dma_start(ring_rows[:, slot, :], None, table[:, :],
                                                    bass.IndirectOffsetOnAxis(rowid[:, s, j:j + 1], 0)
                                                    ).then_inc(arrived[slot], 16)

                with pool.Fori(0, TILES) as t:
                    pool.wait_ge(chosen_ready, t + 1)
                    settle(pool, passed)
                    with pool.Fori(0, PEER_HEADS // 2) as pair:
                        for s in range(2):
                            step(t, t * PEER_HEADS + pair * 2 + s, s)

            def slot_value(g, j):
                return 16 * (g * (TOPK // RING) + j // RING + 1)

            @block.vector
            def _(dve):
                def top16(sets, values, to, to_index, done):
                    def stage(operation, signal=None):
                        for i in range(sets):
                            last = operation(i)
                        signal(last) if signal else topk.add(last)
                        if not signal:
                            topk.wait(dve)
                            settle(dve, passed)
                    settle(dve, passed)
                    stage(lambda i: nc.vector.max(to[:, i, 0:8], values[:, i, :]))
                    stage(lambda i: nc.vector.max_index(to_index[:, i, 0:8], to[:, i, 0:8], values[:, i, :]))
                    stage(lambda i: nc.vector.match_replace(values[:, i, :], to[:, i, 0:8], values[:, i, :], LOWEST))
                    stage(lambda i: nc.vector.max(to[:, i, 8:16], values[:, i, :]))
                    stage(lambda i: nc.vector.max_index(to_index[:, i, 8:16], to[:, i, 8:16], values[:, i, :]), done)

                def search(t, c):
                    if c == 0:
                        topk.begin(t)
                    ring.emptied(dve, t, 3 * c + SCORE)
                    top16(CS, scores, top[:, c * CS:(c + 1) * CS, :], topi[:, c * CS:(c + 1) * CS, :],
                          lambda last: last.then_inc(scores_used, 1))

                def pair_up(t):
                    dve.wait_ge(scores_used, CHUNKS * (t + 1))
                    pairs = top[:, :, :].rearrange("p (h i) k -> p h i k", i=2)
                    nc.vector.tensor_copy(topf[:, :, :], topi[:, :, :])
                    topk.add(nc.vector.tensor_tensor(
                        cand4, pairs[:, :, 0, :].unsqueeze(3).to_broadcast([P, PEER_HEADS, TOPK, TOPK]),
                        pairs[:, :, 1, :].unsqueeze(2).to_broadcast([P, PEER_HEADS, TOPK, TOPK]), ALU.add))
                    topk.wait(dve)
                    top16(PEER_HEADS, cand3, best, pos, topk.add)
                    topk.wait(dve)
                    nc.vector.tensor_tensor(shifted[:, :].rearrange("p (h k) -> p h k", h=PEER_HEADS), best[:, :, :],
                                            best[:, :, 0:1].to_broadcast([P, PEER_HEADS, TOPK]), ALU.subtract
                                            ).then_inc(shifted_ready, 1)

                def name_experts(t):
                    flat = pos[:, :, :].rearrange("p h k -> p (h k)")
                    nc.vector.tensor_scalar(half_pos[:, 0, :], flat, 4, None, ALU.logical_shift_right)
                    topk.add(nc.vector.tensor_scalar(half_pos[:, 1, :], flat, 15, None, ALU.bitwise_and))
                    topk.wait(dve)
                    topk.add(nc.vector.tensor_copy(half_f[:, :, :, :].rearrange("p i h k -> p (i h k)"),
                                                   half_pos[:, :, :].rearrange("p i n -> p (i n)")))
                    topk.wait(dve)
                    keys = topf[:, :, :].rearrange("p (h i) k -> p h i k", i=2)
                    for i in range(2):
                        topk.add(nc.vector.tensor_tensor(
                            hit3, half_f[:, i, :, :].rearrange("p h k -> p (h k)").unsqueeze(2).to_broadcast([P, HK, TOPK]),
                            iota_sb[:, :].unsqueeze(1).to_broadcast([P, HK, TOPK]), ALU.is_equal))
                        topk.wait(dve)
                        topk.add(nc.vector.tensor_tensor(
                            hit4, hit4, keys[:, :, i, :].unsqueeze(2).to_broadcast([P, PEER_HEADS, TOPK, TOPK]),
                            ALU.mult))
                        topk.wait(dve)
                        topk.add(nc.vector.reduce_sum(found[:, i, :], hit3, AX.X))
                        topk.wait(dve)
                    nc.vector.scalar_tensor_tensor(out=chosen[:, bass.ds(t * HK, HK)], in0=found[:, 0, :],
                                                   scalar=float(N_KEYS), in1=found[:, 1, :],
                                                   op0=ALU.mult, op1=ALU.add).then_inc(chosen_ready, 1)

                def normalise(t):
                    dve.wait_ge(wexp_ready, t + 1)
                    topk.add(nc.vector.reduce_sum(wsum[:, :], shifted[:, :].rearrange("p (h k) -> p h k", h=PEER_HEADS),
                                                  AX.X))
                    topk.wait(dve)
                    topk.add(nc.vector.reciprocal(rwsum[:, :], wsum[:, :]))
                    topk.wait(dve)
                    nc.vector.tensor_tensor(
                        weight[:, bass.ds(t * HK, HK)].rearrange("p (h k) -> p h k", h=PEER_HEADS),
                        shifted[:, :].rearrange("p (h k) -> p h k", h=PEER_HEADS),
                        rwsum[:, :].unsqueeze(2).to_broadcast([P, PEER_HEADS, TOPK]), ALU.mult).then_inc(weight_ready, 1)
                    assert topk.n == topk.per, topk.n

                def route_slice(t, c):
                    if c < CHUNKS:
                        search(t, c)
                    elif c == CHUNKS:
                        pair_up(t)
                    elif c == CHUNKS + 1:
                        name_experts(t)
                    elif c == CHUNKS + 2:
                        normalise(t)

                def start(t):
                    dve.wait_ge(h2n_in, 16 * t + 16)
                    nc.vector.tensor_copy(h2_now, h2_next).then_inc(h2_copied, 1)
                    dve.wait_ge(weight_ready, t + 1)
                    dve.wait_ge(h2_copied, t + 1)

                def step(t, g, s, route, first):
                    for j in range(TOPK):
                        slot = j % RING
                        dve.wait_ge(u_in[slot], slot_value(g, j))
                        nc.vector.tensor_tensor_reduce(out=u_rows[:, slot, :], in0=u_rows[:, slot, :], in1=h2_now,
                                                       scale=1.0, scalar=0.0, op0=ALU.mult, op1=ALU.add,
                                                       accum_out=dots[:, s, j:j + 1]).then_inc(u_used, 1)
                    dve.wait_ge(gelu_ready, g + 1)
                    nc.vector.tensor_tensor(coef[:, s, :], gelu[:, s, :], weight[:, bass.ds(g * TOPK, TOPK)], ALU.mult
                                            ).then_inc(coef_ready, 1)
                    route()

                def end(t):
                    dve.wait_ge(v_used, RING + HK * (t + 1))
                    dve.wait_ge(x1n_in, 16 * t + 16)
                    dve.wait_ge(rstd_ready, t + 1)
                    for c in range(2):
                        part = slice(c * BANK, (c + 1) * BANK)
                        nc.vector.tensor_tensor(x2[:, part], acc[c][:, :], x1_now[:, part], ALU.add).then_inc(x2_ready, 1)
                    dve.wait_ge(rms_ready, t + 1)
                    nc.vector.reciprocal(small[:, 2:3], small[:, 1:2]).then_inc(rstd_ready, 1)
                    dve.wait_ge(rstd_ready, t + 2)
                    nc.vector.scalar_tensor_tensor(out=y, in0=x2, scalar=small[:, 2:3], in1=gain[:, :],
                                                   op0=ALU.mult, op1=ALU.mult).then_inc(y_ready, 1)

                dve.sem_inc(u_used, RING)
                dve.sem_inc(x2_ready, 2)
                dve.sem_inc(rstd_ready, 1)
                dve.sem_inc(y_free, 1)
                dve.wait_ge(egain_in, 16)
                dve.wait_ge(rconst_in, 32)
                experts_with_route(dve, start, step, end, route_slice)

            @block.scalar
            def _(act):
                def route_slice(t, c):
                    if c < CHUNKS:
                        for use, to in ((QUERY, q_sb), (QUERYT, qT.rearrange("p s n -> p (s n)")),
                                        (SCORE, scores[:, :, :].rearrange("p s n -> p (s n)"))):
                            bank = ring.filled(act, t, 3 * c + use)
                            if use == SCORE:
                                after(act, scores_used, CHUNKS * t + c)
                            nc.scalar.activation(to, bank[:, :], ACT.Copy).then_inc(ring.free, 1)
                    elif c == CHUNKS + 1:
                        act.wait_ge(shifted_ready, t + 1)
                        nc.scalar.activation(shifted[:, :], shifted[:, :], ACT.Exp).then_inc(wexp_ready, 1)

                def step(t, g, s, route, first):
                    route()
                    act.wait_ge(u_used, RING + TOPK * (g + 1))
                    nc.scalar.activation(gelu[:, s, :], dots[:, s, :], ACT.Gelu).then_inc(gelu_ready, 1)
                    act.wait_ge(coef_ready, g + 1)
                    for j in range(TOPK):
                        act.wait_ge(v_used, g * TOPK + j + 1 + RING - DIAGS)
                        nc.scalar.activation(diag[:, j % DIAGS, :], ident[:, :], ACT.Copy, scale=coef[:, s, j:j + 1]
                                             ).then_inc(diag_ready, 1)

                def end(t):
                    act.wait_ge(x2_ready, 2 * t + 4)
                    act.wait_ge(y_free, t + 1)
                    nc.scalar.activation(y, x2, ACT.Square, accum_out=small[:, 0:1]).then_inc(sumsq_ready, 1)
                    act.wait_ge(sumsq_ready, t + 1)
                    nc.scalar.activation(small[:, 1:2], small[:, 0:1], ACT.Sqrt, bias=small[:, 14:15],
                                         scale=1.0 / D).then_inc(rms_ready, 1)

                ring.open(act)
                experts_with_route(act, nothing, step, end, route_slice)

            @block.tensor
            def _(pe):
                def route_slice(t, c):
                    if c >= CHUNKS:
                        return
                    if c == 0:
                        pe.wait_ge(h2T_in, 16 * t + 16)
                    bank = ring.claim(pe, t, 3 * c + QUERY)
                    for k in range(KC):
                        last = nc.tensor.matmul(bank[:, :], h2T[:, k * P:(k + 1) * P],
                                                wq_sb[:, k, c * BANK:(c + 1) * BANK],
                                                start=(k == 0), stop=(k == KC - 1))
                    last.then_inc(ring.full, 1)
                    ring.emptied(pe, t, 3 * c + QUERY)
                    bank = ring.claim(pe, t, 3 * c + QUERYT)
                    for i in range(CS):
                        last = nc.tensor.transpose(bank[:, i * P:(i + 1) * P], q_sb[:, i * P:(i + 1) * P], ident[:, :])
                    last.then_inc(ring.full, 1)
                    ring.emptied(pe, t, 3 * c + QUERYT)
                    bank = ring.claim(pe, t, 3 * c + SCORE)
                    for i in range(CS):
                        last = nc.tensor.matmul(bank[:, i * P:(i + 1) * P], qT[:, i, :], sk_sb[:, c * CS + i, :],
                                                start=True, stop=True)
                    last.then_inc(ring.full, 1)

                def start(t):
                    pe.wait_ge(x2_ready, 2 * t + 2)

                def step(t, g, s, route, first):
                    route()
                    for j in range(TOPK):
                        slot = j % RING
                        pe.wait_ge(diag_ready, g * TOPK + j + 1)
                        pe.wait_ge(v_in[slot], slot_value(g, j))
                        for c in range(2):
                            last = nc.tensor.matmul(acc[c][:, :], diag[:, j % DIAGS, :],
                                                    v_rows[:, slot, c * BANK:(c + 1) * BANK],
                                                    start=(first and j == 0), stop=True, skip_group_check=True)
                        last.then_inc(v_used, 1)

                pe.sem_inc(v_used, RING)
                pe.wait_ge(wq_in, 16)
                pe.wait_ge(rconst_in, 32)
                experts_with_route(pe, start, step, nothing, route_slice)


_INS = ["x", "norm1_g", "w_in", "sink_logits", "pool_w", "pool_scale", "w_branch", "w_gate", "b_gate", "w_out",
        "norm2_g", "peer_w_query", "peer_sub_keys", "peer_u", "peer_v", "norm_final_g"]


def _constants(S):
    import numpy as np
    q, c = np.arange(P)[:, None], np.arange(3 * P)[None, :]
    dist = np.abs(q + P - c).astype(np.float32)
    slopes = np.array([2.0 ** (-8.0 * (h + 1) / QH) for h in range(QH)], np.float32)
    tiles = S // P
    windows = (2, 4, 8, 16)
    table = np.zeros((tiles, P, QH * 3 * P + GROUPS), np.float32)
    for t in range(tiles):
        s_abs = (t - 1) * P + c
        valid = (dist <= P) & (s_abs >= 0) & (s_abs < S)
        bias = np.where(valid[None], -slopes[:, None, None] * dist[None], np.float32(-1e30))
        table[t, :, :QH * 3 * P] = bias.transpose(1, 0, 2).reshape(P, -1)
        for g, w in enumerate(windows):
            at = t * P + np.arange(P)
            n = np.clip(at + w - w // 2, 0, S) - np.clip(at - w // 2, 0, S)
            table[t, :, QH * 3 * P + g] = np.float32(1.0) / n.astype(np.float32)
    band = np.zeros((P, 3, GROUPS, P), np.float32)
    s, t = np.arange(P)[:, None], np.arange(P)[None, :]
    for b in range(3):
        for g, w in enumerate(windows):
            d = s + (b - 1) * P - t
            band[:, b, g, :] = (d >= -(w // 2)) & (d < w - w // 2)
    return {"identity": np.eye(P, dtype=np.float32), "band": band,
            "bias_table": table.reshape(tiles * P, -1),
            "iota16": np.tile(np.arange(TOPK, dtype=np.float32), (P, 1))}


def kernel(**inputs):
    import numpy as np
    import concourse.bacc as bacc
    from concourse.bass_utils import run_bass_kernel_spmd

    a = {n: np.asarray(inputs[n]) for n in _INS}
    S, D = a["x"].shape[1:]
    lay = {
        "x": a["x"][0], "norm1_g": a["norm1_g"][0], "w_in": a["w_in"][0], "sink_logits": a["sink_logits"][0],
        "pool_w": a["pool_w"][0], "pool_scale": a["pool_scale"][0].reshape(GROUPS, P).T,
        "w_branch": a["w_branch"][0].reshape(-1, D), "w_gate": a["w_gate"][0], "b_gate": a["b_gate"][0],
        "w_out": a["w_out"][0], "norm2_g": a["norm2_g"][0], "w_query": a["peer_w_query"][0],
        "sub_keys_t": a["peer_sub_keys"][0].transpose(3, 0, 1, 2).reshape(P, PEER_HEADS * 2, N_KEYS),
        "peer_u": a["peer_u"][0], "peer_v": a["peer_v"][0], "norm_final_g": a["norm_final_g"],
    }
    lay.update(_constants(S))
    nc = bacc.Bacc("TRN2", target_bir_lowering=False, num_devices=1)
    arrays, args = {}, {}
    for name, value in lay.items():
        arrays[f"in_{name}"] = np.ascontiguousarray(value)
        args[name] = nc.dram_tensor(f"in_{name}", value.shape, mybir.dt.from_np(value.dtype), kind="ExternalInput").ap()
    out = nc.dram_tensor("out_0", (S, D), F32, kind="ExternalOutput").ap()
    encoder_block(nc, out=out, **args)
    r = run_bass_kernel_spmd(nc, [arrays], core_ids=[0])
    return r.results[0]["out_0"].reshape(1, S, D)
```

```python
from contextlib import ExitStack

import concourse.bass as bass
from concourse import mybir

F32 = mybir.dt.float32
U32 = mybir.dt.uint32
ALU = mybir.AluOpType
ACT = mybir.ActivationFunctionType
AX = mybir.AxisListType

P = 128
EPS = 1e-6
LOWEST = -3.4028234663852886e38
HEAD_DIM = 64
QH = 8
KVH = 2
GROUPS = 4
PEER_HEADS = 8
TOPK = 16
N_KEYS = 128
BANK = 512
RING = 8


class Steps:

    def __init__(self, sem, per):
        self.sem, self.per, self.base, self.n = sem, per, 0, 0

    def begin(self, t):
        self.base, self.n = t * self.per, 0

    def add(self, instruction):
        self.n += 1
        assert self.n <= self.per
        return instruction.then_inc(self.sem, 1)

    def wait(self, engine):
        engine.wait_ge(self.sem, self.base + self.n)


def settle(engine, passed):
    engine.sem_inc(passed, 1)


def after(engine, sem, value):
    if not (isinstance(value, int) and value <= 0):
        engine.wait_ge(sem, value)


def every_tile(engine, tiles, body):
    body(0, False)
    with engine.Fori(1, tiles - 1) as t:
        body(t, False)
    body(tiles - 1, True)


class Ring:

    def __init__(self, banks, full, free, per):
        assert per % len(banks) == 0
        self.banks, self.full, self.free, self.per = banks, full, free, per

    def open(self, engine):
        engine.sem_inc(self.free, len(self.banks))

    def bank(self, k):
        return self.banks[k % len(self.banks)]

    def claim(self, engine, t, k):
        engine.wait_ge(self.free, t * self.per + k + 1)
        return self.bank(k)

    def filled(self, engine, t, k):
        after(engine, self.full, t * self.per + k + 1)
        return self.bank(k)

    def emptied(self, engine, t, k):
        engine.wait_ge(self.free, t * self.per + k + 1 + len(self.banks))


def encoder_block(nc, x, norm1_g, w_in, sink_logits, pool_w, pool_scale, w_branch, w_gate, b_gate,
                  w_out, norm2_g, w_query, sub_keys_t, peer_u, peer_v, norm_final_g,
                  identity, band, bias_table, iota16, out):
    S, D = x.shape
    TILES = S // P
    KC = D // P
    ATT = QH * HEAD_DIM
    KVW = KVH * HEAD_DIM
    PW = D // 2
    AC = ATT // P
    CW = 3 * P
    BW = QH * CW + GROUPS
    SETS = PEER_HEADS * 2
    HK = PEER_HEADS * TOPK

    qT_d = nc.dram_tensor("qT_scratch", (S, ATT), F32, kind="Internal").ap()
    kT_d = nc.dram_tensor("kT_scratch", (S + 2 * P, P), F32, kind="Internal").ap()
    v_d = nc.dram_tensor("v_scratch", (S + 2 * P, KVW), F32, kind="Internal").ap()
    u_d = nc.dram_tensor("u_scratch", (S + 2 * P, PW), F32, kind="Internal").ap()
    gate_d = nc.dram_tensor("gate_scratch", (S, 2 * D), F32, kind="Internal").ap()
    x1_d = nc.dram_tensor("x1_scratch", (S, D), F32, kind="Internal").ap()

    def rows(t, n=1):
        return bass.ds(t * P, n * P)

    with ExitStack() as ctx:
        def sem(name):
            return ctx.enter_context(nc.semaphore(name))

        psum = [ctx.enter_context(nc.psum_tensor(f"bank{i}", [P, BANK], F32)) for i in range(8)]

        def keep(name, shape, dt=F32):
            return ctx.enter_context(nc.sbuf_tensor(name, shape, dt))

        ident = keep("ident", [P, P])
        gain = keep("gain", [P, D])
        small = keep("small", [P, 16])

        region1 = keep("region1", [P, 10240])
        chosen = region1[:, RING * D:RING * D + TILES * HK].bitcast(U32)
        region2 = keep("region2", [P, 16384])
        region3 = keep("region3", [P, 16384])

        def carve(region):
            at = [0]

            def take(n, dt=F32):
                at[0] += n
                assert at[0] <= region.shape[1], at
                return region[:, at[0] - n:at[0]] if dt is F32 else region[:, at[0] - n:at[0]].bitcast(dt)
            return take

        win_sb = region1[:, 0:KC * 1280].rearrange("p (k n) -> p k n", k=KC)
        wg_sb = region2[:, :].rearrange("p (k n) -> p k n", k=KC)
        wb_sb = region3[:, 0:2 * AC * D].rearrange("p (b k n) -> p b k n", b=2, k=AC)
        wo_sb = region3[:, 2 * AC * D:].rearrange("p (k n) -> p k n", k=KC)
        wq_sb = region2[:, :].rearrange("p (k n) -> p k n", k=KC)

        const_in = sem("const_in")
        IN_PARTS = ((0, ATT), (ATT, 2 * KVW), (ATT + 2 * KVW, PW))
        GCH = 2 * D // BANK
        win_in = [sem(f"win_in{i}") for i in range(len(IN_PARTS))]
        wg_in = [sem(f"wg_in{c}") for c in range(GCH)]
        bg_in = sem("b_gate_in")
        wbo_in = sem("wbo_in")
        wq_in = sem("wq_in")
        gain2_in = sem("norm2_gain_in")
        eps_ready = sem("eps_ready")
        passed = sem("waits_passed")

        with ExitStack() as pctx:
            def tmp(name, shape, dt=F32):
                return pctx.enter_context(nc.sbuf_tensor(name, shape, dt))
            xin = tmp("xin", [P, D])
            h = tmp("h", [P, D])
            hT = tmp("hT", [P, KC, P])
            gates = region3[:, 0:2 * D]
            bg = region3[:, 2 * D:4 * D]
            zeros = region3[:, 4 * D:4 * D + PW]
            q_sb = tmp("q_sb", [P, ATT])
            k_sb = tmp("k_sb", [P, P])
            v_sb = tmp("v_sb", [P, KVW])
            u_sb = tmp("u_sb", [P, PW])
            qT = tmp("qT_out", [P, ATT])
            kT = tmp("kT_out", [P, P])
            x_in = sem("x_in")
            sumsq_ready = sem("sumsq_ready")
            rms_ready = sem("rms_ready")
            rstd_ready = sem("rstd_ready")
            h_ready = sem("h_ready")
            by_act = Ring(psum[0:2], sem("project_act_full"), sem("project_act_free"), 6)
            by_dve = Ring(psum[2:7], sem("project_dve_full"), sem("project_dve_free"), 5)
            v_ready = sem("v_ready")
            gate_ready = sem("gate_ready")
            zero_ready = sem("zero_ready")
            pads_out = sem("pads_out")
            qT_out, kT_out, v_out, u_out, g_out = (
                sem(n) for n in ("qT_stored", "kT_stored", "v_stored", "u_stored", "gates_stored"))
            HT, Q, KV, QT, KT = 0, 2, 3, 4, 5
            U, G = 0, 1

            with nc.Block() as block:
                @block.sync
                def _(sp):
                    sp.dma_start(xin[:, :], x[0:P, :]).then_inc(x_in, 16)
                    sp.dma_start(ident[:, :], identity).then_inc(const_in, 16)
                    sp.dma_start(gain[:, :], norm1_g.partition_broadcast(P)).then_inc(const_in, 16)
                    for use, (at, n) in enumerate(IN_PARTS):
                        sp.dma_start(win_sb[:, :, at:at + n], w_in[:, at:at + n].rearrange("(k p) n -> p k n", p=P)
                                     ).then_inc(win_in[use], 16)
                    sp.dma_start(bg, b_gate.partition_broadcast(P)).then_inc(bg_in, 16)
                    for c in range(GCH):
                        part = slice(c * BANK, (c + 1) * BANK)
                        sp.dma_start(wg_sb[:, :, part], w_gate[:, part].rearrange("(k p) n -> p k n", p=P)
                                     ).then_inc(wg_in[c], 16)
                    with sp.Fori(1, TILES) as t:
                        sp.wait_ge(h_ready, t)
                        sp.dma_start(xin[:, :], x[rows(t), :]).then_inc(x_in, 16)
                    sp.dma_start(wo_sb, w_out.rearrange("(k p) n -> p k n", p=P)).then_inc(wbo_in, 16)
                    sp.wait_ge(pads_out, 6 * 16)
                    sp.dma_start(wb_sb[:, 1, :, :], w_branch[ATT:, :].rearrange("(k p) n -> p k n", p=P)
                                 ).then_inc(wbo_in, 16)

                @block.gpsimd
                def _(pool):
                    nc.gpsimd.memset(zeros, 0.0).then_inc(zero_ready, 1)
                    pool.wait_ge(zero_ready, 1)
                    for at in (0, S + P):
                        pool.dma_start(kT_d[at:at + P, :], zeros[:, 0:P]).then_inc(pads_out, 16)
                        pool.dma_start(v_d[at:at + P, :], zeros[:, 0:KVW]).then_inc(pads_out, 16)
                        pool.dma_start(u_d[at:at + P, :], zeros).then_inc(pads_out, 16)
                    with pool.Fori(0, TILES) as t:
                        pool.wait_ge(v_ready, t + 1)
                        settle(pool, passed)
                        pool.dma_start(v_d[rows(t + 1), :], v_sb[:, :]).then_inc(v_out, 16)
                        by_dve.emptied(pool, t, U)
                        settle(pool, passed)
                        pool.dma_start(u_d[rows(t + 1), :], u_sb[:, :]).then_inc(u_out, 16)
                        by_act.emptied(pool, t, QT)
                        settle(pool, passed)
                        pool.dma_start(qT_d[rows(t), :], qT[:, :]).then_inc(qT_out, 16)
                        by_act.emptied(pool, t, KT)
                        settle(pool, passed)
                        pool.dma_start(kT_d[rows(t + 1), :], kT[:, :]).then_inc(kT_out, 16)
                        pool.wait_ge(gate_ready, t + 1)
                        settle(pool, passed)
                        pool.dma_start(gate_d[rows(t), :], gates).then_inc(g_out, 16)
                    pool.wait_ge(pads_out, 6 * 16)
                    for stored in (qT_out, kT_out, v_out, u_out):
                        pool.wait_ge(stored, 16 * TILES)

                @block.scalar
                def _(act):
                    by_act.open(act)
                    act.wait_ge(eps_ready, 1)
                    def measure(t):
                        act.wait_ge(x_in, 16 * t + 16)
                        after(act, rstd_ready, t)
                        nc.scalar.activation(h[:, :], xin[:, :], ACT.Square, accum_out=small[:, 0:1]
                                             ).then_inc(sumsq_ready, 1)
                        act.wait_ge(sumsq_ready, t + 1)
                        nc.scalar.activation(small[:, 1:2], small[:, 0:1], ACT.Sqrt, bias=small[:, 14:15],
                                             scale=1.0 / D).then_inc(rms_ready, 1)

                    def body(t, last):
                        by_dve.filled(act, t, -1)
                        for half in range(2):
                            bank = by_act.filled(act, t, HT + half)
                            nc.scalar.activation(hT[:, 4 * half:4 * half + 4, :],
                                                 bank[:, :].rearrange("p (k n) -> p k n", k=4),
                                                 ACT.Copy).then_inc(by_act.free, 1)
                        bank = by_act.filled(act, t, Q)
                        nc.scalar.activation(q_sb[:, :].rearrange("p (c g d) -> p g c d", c=4, g=KVH),
                                             bank[:, :].rearrange("p (g c d) -> p g c d", g=KVH, c=4),
                                             ACT.Copy).then_inc(by_act.free, 1)
                        bank = by_act.filled(act, t, KV)
                        after(act, v_out, 16 * t)
                        nc.scalar.activation(v_sb[:, :], bank[:, P:P + KVW], ACT.Copy).then_inc(v_ready, 1)
                        nc.scalar.activation(k_sb[:, :], bank[:, 0:P], ACT.Copy).then_inc(by_act.free, 1)
                        bank = by_act.filled(act, t, QT)
                        after(act, qT_out, 16 * t)
                        nc.scalar.activation(qT[:, :], bank[:, :], ACT.Copy).then_inc(by_act.free, 1)
                        bank = by_act.filled(act, t, KT)
                        after(act, kT_out, 16 * t)
                        nc.scalar.activation(kT[:, :], bank[:, 0:P], ACT.Copy).then_inc(by_act.free, 1)
                        if not last:
                            measure(t + 1)
                        by_dve.emptied(act, t, G + GCH - 1)
                        nc.scalar.activation(gates, gates, ACT.Sigmoid).then_inc(gate_ready, 1)

                    measure(0)
                    every_tile(act, TILES, body)

                @block.vector
                def _(dve):
                    by_dve.open(dve)
                    nc.vector.memset(small[:, 14:15], EPS).then_inc(eps_ready, 1)
                    dve.wait_ge(const_in, 32)
                    def normalise(t):
                        dve.wait_ge(rms_ready, t + 1)
                        nc.vector.reciprocal(small[:, 2:3], small[:, 1:2]).then_inc(rstd_ready, 1)
                        dve.wait_ge(rstd_ready, t + 1)
                        nc.vector.scalar_tensor_tensor(out=h[:, :], in0=xin[:, :], scalar=small[:, 2:3],
                                                       in1=gain[:, :], op0=ALU.mult, op1=ALU.mult
                                                       ).then_inc(h_ready, 1)

                    def body(t, last):
                        bank = by_dve.filled(dve, t, U)
                        after(dve, u_out, 16 * t)
                        nc.vector.tensor_copy(u_sb[:, :], bank[:, :]).then_inc(by_dve.free, 1)
                        if not last:
                            by_act.filled(dve, t, HT + 1)
                            normalise(t + 1)
                        after(dve, g_out, 16 * t)
                        dve.wait_ge(bg_in, 16)
                        for c in range(GCH):
                            bank = by_dve.filled(dve, t, G + c)
                            part = slice(c * BANK, (c + 1) * BANK)
                            nc.vector.tensor_tensor(gates[:, part], bank[:, :], bg[:, part], ALU.add
                                                    ).then_inc(by_dve.free, 1)

                    normalise(0)
                    every_tile(dve, TILES, body)

                @block.tensor
                def _(pe):
                    def project(t, ring, use, w, n):
                        bank = ring.claim(pe, t, use)
                        for k in range(KC):
                            last = nc.tensor.matmul(bank[:, 0:n], hT[:, k, :], w[:, k, :],
                                                    start=(k == 0), stop=(k == KC - 1))
                        last.then_inc(ring.full, 1)

                    pe.wait_ge(const_in, 32)
                    with pe.Fori(0, TILES) as t:
                        pe.wait_ge(h_ready, t + 1)
                        for half in range(2):
                            bank = by_act.claim(pe, t, HT + half)
                            for k in range(4):
                                c = (4 * half + k) * P
                                last = nc.tensor.transpose(bank[:, k * P:(k + 1) * P], h[:, c:c + P], ident[:, :])
                            last.then_inc(by_act.full, 1)
                        by_act.emptied(pe, t, HT + 1)
                        for (ring, use), arrived, (at, n) in zip(((by_act, Q), (by_act, KV), (by_dve, U)),
                                                                 win_in, IN_PARTS):
                            pe.wait_ge(arrived, 16)
                            project(t, ring, use, win_sb[:, :, at:at + n], n)
                        bank = by_act.claim(pe, t, QT)
                        for c in range(AC):
                            last = nc.tensor.transpose(bank[:, c * P:(c + 1) * P], q_sb[:, c * P:(c + 1) * P],
                                                       ident[:, :])
                        last.then_inc(by_act.full, 1)
                        bank = by_act.claim(pe, t, KT)
                        nc.tensor.transpose(bank[:, 0:P], k_sb[:, :], ident[:, :]).then_inc(by_act.full, 1)
                        for c in range(GCH):
                            pe.wait_ge(wg_in[c], 16)
                            project(t, by_dve, G + c, wg_sb[:, :, c * BANK:(c + 1) * BANK], BANK)

        with ExitStack() as mctx:
            def tmp(name, shape, dt=F32):
                return mctx.enter_context(nc.sbuf_tensor(name, shape, dt))
            take = carve(region1)
            bias = take(BW)
            L = bias[:, 0:QH * CW].rearrange("p (h c) -> p h c", h=QH)
            rcount = bias[:, QH * CW:BW]
            qT = take(ATT).rearrange("p (c n) -> p c n", c=4)
            kw = take(CW).rearrange("p (b n) -> p b n", b=3)
            vw = take(3 * KVW).rearrange("p (b n) -> p b n", b=3)
            uw = take(3 * PW).rearrange("p (b n) -> p b n", b=3)
            PT = take(2 * CW).rearrange("p (s b n) -> p s b n", s=2, b=3)
            o_sb = take(ATT)
            oT = take(ATT).rearrange("p (k n) -> p k n", k=AC)
            mixed = take(PW)
            mixedT = take(PW).rearrange("p (g n) -> p g n", g=GROUPS)
            opT = take(PW).rearrange("p (k n) -> p k n", k=AC)
            gates = tmp("gates_in", [P, 2 * D])
            xres = tmp("xres", [P, D])
            mT = tmp("mT", [P, KC, P])
            x1 = tmp("x1", [P, D])
            band_sb = tmp("band_sb", [P, 3, GROUPS, P])
            pw_sb = take(GROUPS * P).rearrange("p (g n) -> p g n", g=GROUPS)
            ps_sb = tmp("ps_sb", [P, GROUPS])
            sink = tmp("sink", [P, QH])
            nsink = tmp("nsink", [P, QH])
            nmax = tmp("nmax", [P, QH])
            nshift = tmp("nshift", [P, QH])
            sdiff = tmp("sdiff", [P, QH])
            sexp = tmp("sexp", [P, QH])
            rsum = tmp("rsum", [P, QH])
            den = tmp("den", [P, QH])
            rden = tmp("rden", [P, QH])
            mconst_in, sink_in, nsink_ready = sem("mix_const_in"), sem("sink_in"), sem("nsink_ready")
            bias_in, qk_in, vu_in, gx_in = sem("bias_in"), sem("qk_in"), sem("vu_in"), sem("gx_in")
            shift_ready, exp_ready = sem("shift_ready"), sem("exp_ready")
            rden_ready, pv_done = sem("rden_ready"), sem("pv_done")
            softmax = Steps(sem("softmax_steps"), 4)
            merged_ready = sem("merged_ready")
            x1_out = sem("x1_stored")
            a_dve = Ring(psum[0:2], sem("a_dve_full"), sem("a_dve_free"), 12)
            a_act = Ring(psum[2:4], sem("a_act_full"), sem("a_act_free"), 10)
            b_dve = Ring(psum[4:6], sem("b_dve_full"), sem("b_dve_free"), 6)
            b_act = Ring(psum[6:8], sem("b_act_full"), sem("b_act_free"), 2)
            LOGITS, POOLED, ATTN, MIXED = 0, 8, 9, 10
            PTR, MIXEDT, OT = 0, 8, 9
            BRANCH, OUT = 0, 4
            MT = 0
            EXPS = QH + 1

            def pipeline(engine, attend, branch, weigh, output, finish):
                def stages(t, now=True, before=True):
                    if now:
                        attend(t)
                    if before:
                        branch(t - 1)
                    if now:
                        weigh(t)
                    if before:
                        output(t - 1)
                    if now:
                        finish(t)

                for t in range(2):
                    stages(t, before=t > 0)
                with engine.Fori(2, TILES) as t:
                    stages(t)
                stages(TILES, now=False)

            with nc.Block() as block:
                @block.sync
                def _(sp):
                    def attend(t, first=False):
                        if not first:
                            a_act.filled(sp, t - 1, PTR + QH - 1)
                            a_dve.emptied(sp, t - 1, POOLED)
                        sp.dma_start(qT, qT_d[rows(t), :].rearrange("p (c n) -> p c n", c=4)).then_inc(qk_in, 16)
                        sp.dma_start(kw, kT_d[rows(t, 3), :].rearrange("(b p) n -> p b n", p=P)).then_inc(qk_in, 16)
                        sp.dma_start(bias, bias_table[rows(t), :]).then_inc(bias_in, 16)
                        if first:
                            sp.dma_start(sink[:, :], sink_logits.partition_broadcast(P)).then_inc(sink_in, 16)
                            sp.dma_start(band_sb[:, :, :, :], band).then_inc(mconst_in, 16)
                        else:
                            a_dve.filled(sp, t - 1, ATTN)
                        sp.dma_start(vw, v_d[rows(t, 3), :].rearrange("(b p) n -> p b n", p=P)).then_inc(vu_in, 16)
                        sp.dma_start(uw, u_d[rows(t, 3), :].rearrange("(b p) n -> p b n", p=P)).then_inc(vu_in, 16)

                    def merge(t, first=False):
                        if not first:
                            b_dve.emptied(sp, t - 1, OUT + 1)
                            b_act.filled(sp, t - 1, MT + 1)
                        sp.dma_start(gates[:, :], gate_d[rows(t), :]).then_inc(gx_in, 16)
                        sp.dma_start(xres[:, :], x[rows(t), :]).then_inc(gx_in, 16)

                    attend(0, True)
                    sp.dma_start(pw_sb, pool_w.rearrange("g c d -> c g d")).then_inc(mconst_in, 16)
                    sp.dma_start(ps_sb[:, :], pool_scale).then_inc(mconst_in, 16)
                    sp.wait_ge(g_out, 16 * TILES)
                    sp.dma_start(wb_sb[:, 0, :, :], w_branch[0:ATT, :].rearrange("(k p) n -> p k n", p=P)
                                 ).then_inc(wbo_in, 16)
                    merge(0, True)
                    attend(1)
                    sp.dma_start(gain[:, :], norm2_g.partition_broadcast(P)).then_inc(gain2_in, 16)
                    sp.dma_start(wq_sb, w_query.rearrange("(k p) n -> p k n", p=P)).then_inc(wq_in, 16)
                    with sp.Fori(2, TILES) as t:
                        attend(t)
                        merge(t - 1)
                    merge(TILES - 1)

                @block.gpsimd
                def _(pool):
                    with pool.Fori(0, TILES) as t:
                        b_dve.emptied(pool, t, OUT + 1)
                        settle(pool, passed)
                        pool.dma_start(x1_d[rows(t), :], x1[:, :]).then_inc(x1_out, 16)
                    pool.wait_ge(x1_out, 16 * TILES)

                @block.tensor
                def _(pe):
                    def attend(t):
                        pe.wait_ge(qk_in, 32 * t + 32)
                        for hd in range(QH):
                            g, c = divmod(hd, 4)
                            half = slice(g * HEAD_DIM, (g + 1) * HEAD_DIM)
                            bank = a_dve.claim(pe, t, LOGITS + hd)
                            nc.tensor.matmul(bank[:, 0:CW], qT[half, c, :],
                                             kw[half, :, :].rearrange("p b n -> p (b n)"), start=True, stop=True
                                             ).then_inc(a_dve.full, 1)
                        pe.wait_ge(vu_in, 32 * t + 32)
                        if isinstance(t, int) and t == 0:
                            pe.wait_ge(mconst_in, 48)
                        bank = a_dve.claim(pe, t, POOLED)
                        for g in range(GROUPS):
                            for b in range(3):
                                last = nc.tensor.matmul(bank[:, g * P:(g + 1) * P], band_sb[:, b, g, :],
                                                        uw[:, b, g * P:(g + 1) * P], start=(b == 0), stop=(b == 2))
                        last.then_inc(a_dve.full, 1)

                    def weigh(t):
                        def weigh_head(hd):
                            a_act.emptied(pe, t, PTR + hd)
                            g = hd // 4
                            for b in range(3):
                                last = nc.tensor.matmul(a_dve.bank(ATTN)[:, hd * HEAD_DIM:(hd + 1) * HEAD_DIM],
                                                        PT[:, hd % 2, b, :],
                                                        vw[:, b, g * HEAD_DIM:(g + 1) * HEAD_DIM],
                                                        start=(b == 0), stop=(b == 2))
                            last.then_inc(pv_done if hd < QH - 1 else a_dve.full, 1)

                        a_dve.claim(pe, t, ATTN)
                        for hd in range(QH):
                            pe.wait_ge(exp_ready, EXPS * t + hd + 1)
                            bank = a_act.claim(pe, t, PTR + hd)
                            for b in range(3):
                                last = nc.tensor.transpose(bank[:, b * P:(b + 1) * P], L[:, hd, b * P:(b + 1) * P],
                                                           ident[:, :])
                            last.then_inc(a_act.full, 1)
                            if hd:
                                weigh_head(hd - 1)
                        weigh_head(QH - 1)
                        a_dve.emptied(pe, t, POOLED)
                        turn(t, MIXEDT, mixed)

                    def turn(t, use, of):
                        bank = a_act.claim(pe, t, use)
                        for c in range(AC):
                            last = nc.tensor.transpose(bank[:, c * P:(c + 1) * P], of[:, c * P:(c + 1) * P],
                                                       ident[:, :])
                        last.then_inc(a_act.full, 1)

                    def finish(t):
                        a_dve.emptied(pe, t, ATTN)
                        turn(t, OT, o_sb)
                        a_act.emptied(pe, t, MIXEDT)
                        for two in range(2):
                            bank = a_dve.claim(pe, t, MIXED + two)
                            for i in range(2):
                                g = 2 * two + i
                                last = nc.tensor.matmul(bank[:, i * P:(i + 1) * P], pw_sb[:, g, :], mixedT[:, g, :],
                                                        start=True, stop=True)
                            last.then_inc(a_dve.full, 1)

                    def branch(t):
                        if isinstance(t, int) and t == 0:
                            pe.wait_ge(wbo_in, 48)
                        a_act.emptied(pe, t, OT)
                        a_dve.emptied(pe, t, MIXED + 1)
                        for c in range(2):
                            for b, of in enumerate((oT, opT)):
                                bank = b_dve.claim(pe, t, BRANCH + 2 * c + b)
                                for k in range(AC):
                                    last = nc.tensor.matmul(bank[:, :], of[:, k, :],
                                                            wb_sb[:, b, k, c * BANK:(c + 1) * BANK],
                                                            start=(k == 0), stop=(k == AC - 1))
                                last.then_inc(b_dve.full, 1)

                    def output(t):
                        for c in range(2):
                            pe.wait_ge(merged_ready, 2 * t + c + 1)
                            bank = b_act.claim(pe, t, MT + c)
                            for k in range(4):
                                at = c * BANK + k * P
                                last = nc.tensor.transpose(bank[:, k * P:(k + 1) * P], gates[:, at:at + P], ident[:, :])
                            last.then_inc(b_act.full, 1)
                        b_act.emptied(pe, t, MT + 1)
                        for c in range(2):
                            bank = b_dve.claim(pe, t, OUT + c)
                            for k in range(KC):
                                last = nc.tensor.matmul(bank[:, :], mT[:, k, :], wo_sb[:, k, c * BANK:(c + 1) * BANK],
                                                        start=(k == 0), stop=(k == KC - 1))
                            last.then_inc(b_dve.full, 1)

                    pipeline(pe, attend, branch, weigh, output, finish)

                @block.scalar
                def _(act):
                    def attend(t):
                        act.wait_ge(shift_ready, 2 * t + 2)
                        for hd in range(QH):
                            nc.scalar.activation(L[:, hd, :], L[:, hd, :], ACT.Exp, bias=nshift[:, hd:hd + 1],
                                                 accum_out=rsum[:, hd:hd + 1]).then_inc(exp_ready, 1)
                        nc.scalar.activation(sexp[:, :], sdiff[:, :], ACT.Exp).then_inc(exp_ready, 1)

                    def weigh(t):
                        for hd in range(QH):
                            bank = a_act.filled(act, t, PTR + hd)
                            if hd >= 2:
                                act.wait_ge(pv_done, (QH - 1) * t + hd - 1)
                            nc.scalar.activation(PT[:, hd % 2, :, :], bank[:, 0:CW].rearrange("p (b n) -> p b n", b=3),
                                                 ACT.Copy).then_inc(a_act.free, 1)
                        turned(t, MIXEDT, mixedT)

                    def turned(t, use, to):
                        bank = a_act.filled(act, t, use)
                        nc.scalar.activation(to, bank[:, :].rearrange("p (k n) -> p k n", k=AC),
                                             ACT.Copy).then_inc(a_act.free, 1)

                    def finish(t):
                        turned(t, OT, oT)

                    def branch(t):
                        pass

                    def output(t):
                        for c in range(2):
                            bank = b_act.filled(act, t, MT + c)
                            nc.scalar.activation(mT[:, 4 * c:4 * c + 4, :], bank[:, :].rearrange("p (k n) -> p k n", k=4),
                                                 ACT.Copy).then_inc(b_act.free, 1)

                    a_act.open(act)
                    b_act.open(act)
                    pipeline(act, attend, branch, weigh, output, finish)

                @block.vector
                def _(dve):
                    def attend(t):
                        softmax.begin(t)
                        dve.wait_ge(bias_in, 16 * t + 16)
                        for hd in range(QH):
                            bank = a_dve.filled(dve, t, LOGITS + hd)
                            nc.vector.scalar_tensor_tensor(out=L[:, hd, :], in0=bank[:, 0:CW], scalar=HEAD_DIM ** -0.5,
                                                           in1=L[:, hd, :], op0=ALU.mult, op1=ALU.add
                                                           ).then_inc(a_dve.free, 1)
                        a_dve.emptied(dve, t, LOGITS + QH - 1)
                        softmax.add(nc.vector.reduce_max(nmax[:, :], L, AX.X, negate=True))
                        softmax.wait(dve)
                        nc.vector.tensor_tensor(nshift[:, :], nmax[:, :], nsink[:, :], ALU.min).then_inc(shift_ready, 1)
                        dve.wait_ge(shift_ready, 2 * t + 1)
                        nc.vector.tensor_tensor(sdiff[:, :], sink[:, :], nshift[:, :], ALU.add).then_inc(shift_ready, 1)
                        bank = a_dve.filled(dve, t, POOLED)
                        for g in range(GROUPS):
                            part = slice(g * P, (g + 1) * P)
                            last = nc.vector.scalar_tensor_tensor(out=mixed[:, part], in0=bank[:, part],
                                                                  scalar=rcount[:, g:g + 1], in1=uw[:, 1, part],
                                                                  op0=ALU.mult, op1=ALU.subtract)
                        last.then_inc(a_dve.free, 1)

                    def weigh(t):
                        dve.wait_ge(exp_ready, EXPS * (t + 1))
                        softmax.add(nc.vector.tensor_tensor(den[:, :], rsum[:, :], sexp[:, :], ALU.add))
                        softmax.wait(dve)
                        softmax.add(nc.vector.reciprocal(rden[:, :], den[:, :]))
                        softmax.wait(dve)
                        bank = a_dve.filled(dve, t, ATTN)
                        nc.vector.tensor_tensor(o_sb.rearrange("p (h d) -> p h d", h=QH),
                                                bank[:, :].rearrange("p (h d) -> p h d", h=QH),
                                                rden[:, :].unsqueeze(2).to_broadcast([P, QH, HEAD_DIM]), ALU.mult
                                                ).then_inc(a_dve.free, 1)
                        softmax.add(nc.vector.memset(small[:, 13:14], 0.0))

                    def finish(t):
                        if isinstance(t, int) and t == 0:
                            dve.wait_ge(mconst_in, 48)
                        for two in range(2):
                            bank = a_dve.filled(dve, t, MIXED + two)
                            nc.vector.tensor_tensor(opT[:, 2 * two:2 * two + 2, :],
                                                    bank[:, 0:2 * P].rearrange("p (g n) -> p g n", g=2),
                                                    ps_sb[:, 2 * two:2 * two + 2].unsqueeze(2).to_broadcast([P, 2, P]),
                                                    ALU.mult).then_inc(a_dve.free, 1)

                    def branch(t):
                        dve.wait_ge(gx_in, 32 * t + 32)
                        for c in range(2):
                            for b in range(2):
                                bank = b_dve.filled(dve, t, BRANCH + 2 * c + b)
                                part = gates[:, b * D + c * BANK:b * D + (c + 1) * BANK]
                                nc.vector.tensor_tensor(part, bank[:, :], part, ALU.mult).then_inc(b_dve.free, 1)
                            b_dve.emptied(dve, t, BRANCH + 2 * c + 1)
                            to = gates[:, c * BANK:(c + 1) * BANK]
                            nc.vector.tensor_tensor(to, to, gates[:, D + c * BANK:D + (c + 1) * BANK], ALU.add
                                                    ).then_inc(merged_ready, 1)

                    def output(t):
                        after(dve, x1_out, 16 * t)
                        for c in range(2):
                            bank = b_dve.filled(dve, t, OUT + c)
                            part = slice(c * BANK, (c + 1) * BANK)
                            nc.vector.tensor_tensor(x1[:, part], bank[:, :], xres[:, part], ALU.add
                                                    ).then_inc(b_dve.free, 1)

                    a_dve.open(dve)
                    b_dve.open(dve)
                    dve.wait_ge(sink_in, 16)
                    nc.vector.tensor_scalar(nsink[:, :], sink[:, :], -1.0, None, ALU.mult).then_inc(nsink_ready, 1)
                    dve.wait_ge(nsink_ready, 1)
                    pipeline(dve, attend, branch, weigh, output, finish)

        def tmp(name, shape, dt=F32):
            return ctx.enter_context(nc.sbuf_tensor(name, shape, dt))
        take = carve(region1)
        u_rows = take(RING * D).rearrange("p (s n) -> p s n", s=RING)
        take = carve(region3)
        v_rows = take(RING * D).rearrange("p (s n) -> p s n", s=RING)
        h2_next, h2_now, x1_now, x2, y = (take(D) for _ in range(5))
        x1_next = tmp("x1_next", [P, D])[:, :]
        final_gain = tmp("final_gain", [P, D])
        sk_sb = take(SETS * N_KEYS).rearrange("p (s n) -> p s n", s=SETS)
        CS = BANK // P
        CHUNKS = SETS // CS
        TOPK_STEPS = 15
        q_sb = take(BANK)
        qT = take(BANK).rearrange("p (s n) -> p s n", s=CS)
        scores = tmp("scores", [P, CS, N_KEYS])
        CH = CS // 2
        CK = CH * TOPK
        cand = tmp("cand", [P, CK * TOPK])
        cand3 = cand[:, :].rearrange("p (h n) -> p h n", h=CH)
        cand4 = cand[:, :].rearrange("p (h a b) -> p h a b", h=CH, a=TOPK)
        hit = tmp("hit", [P, 2 * CK * TOPK])
        hit5 = hit[:, :].rearrange("p (i h k a) -> p i h k a", i=2, h=CH, k=TOPK)
        hit3 = hit[:, :].rearrange("p (n a) -> p n a", a=TOPK)
        top = tmp("top", [P, CS, TOPK])
        topi = tmp("topi", [P, CS, TOPK], U32)
        topf = tmp("topf", [P, CS, TOPK])
        best = tmp("best", [P, CH, TOPK])
        pos = tmp("pos", [P, CH, TOPK], U32)
        half_pos = tmp("half_pos", [P, 2, CK], U32)
        half_f = tmp("half_f", [P, 2 * CK])
        found = tmp("found", [P, 2, CK])
        shifted = tmp("shifted", [P, CK])
        weight = tmp("weight", [P, CK])
        wsum = tmp("wsum", [P, CH])
        rwsum = tmp("rwsum", [P, CH])
        iota_sb = tmp("iota_sb", [P, TOPK])
        h2T = tmp("h2T_in", [P, D])
        DIAGS = 4
        diag = tmp("diag", [P, DIAGS, P])
        dots = tmp("dots", [P, 2, TOPK])
        gelu = tmp("gelu", [P, 2, TOPK])
        coef = tmp("coef", [P, 2, TOPK])
        rowid = tmp("rowid", [P, 2, TOPK], U32)

        keys_in, iota_in = sem("sub_keys_in"), sem("iota_in")
        scores_used = sem("scores_used")
        shifted_ready, wexp_ready = sem("shifted_ready"), sem("wexp_ready")
        chosen_ready, weight_ready = sem("chosen_ready"), sem("weight_ready")
        ring = Ring(psum[2:6], sem("route_full"), sem("route_free"), 3 * CHUNKS)
        turned = Ring(psum[6:8], sem("h2T_full"), sem("h2T_free"), 2)
        QUERY, QUERYT, SCORE = range(3)
        topk = Steps(sem("topk_steps"), TOPK_STEPS)
        normal = Steps(sem("normalise_steps"), 2)
        u_in = [sem(f"u_rows_in{i}") for i in range(RING)]
        v_in = [sem(f"v_rows_in{i}") for i in range(RING)]
        u_used, v_used = sem("u_rows_used"), sem("v_rows_used")
        ids_ready, gelu_ready, coef_ready, diag_ready = (
            sem(n) for n in ("ids_ready", "gelu_ready", "coef_ready", "diag_ready"))
        x1_in, x1_copied, h2_copied = sem("x1_next_in"), sem("x1_copied"), sem("h2_copied")
        sumsq1_ready, rms1_ready, rstd1_ready, h2_ready = (
            sem(n) for n in ("sumsq1_ready", "rms1_ready", "rstd1_ready", "h2_ready"))
        final_gain_in = sem("final_gain_in")
        x2_ready = sem("x2_ready")
        sumsq_ready, rms_ready = sem("sumsq2_ready"), sem("rms2_ready")
        rstd_ready = sem("rstd2_ready")
        y_ready, y_out, y_free = sem("y_ready"), sem("y_stored"), sem("y_free")
        acc = psum[0:2]

        def experts_with_route(engine, start, step, end, measure, norm, search, choose):
            def tile(t, last):
                start(t)
                for hd in range(PEER_HEADS):
                    if hd == PEER_HEADS - CH - 1 and not last:
                        measure(t + 1)
                    if hd == PEER_HEADS - CH and not last:
                        norm(t + 1)
                    ahead, chunk = divmod(hd // CH + 1, CHUNKS)
                    route = choose if hd % CH else search
                    step(t, hd, nothing if last and ahead else lambda: route(t + ahead, chunk))
                end(t)

            measure(0)
            norm(0)
            search(0, 0)
            choose(0, 0)
            with engine.Fori(0, TILES - 1) as t:
                tile(t, False)
            tile(TILES - 1, True)

        def nothing(*_):
            pass

        with nc.Block() as block:
            @block.sync
            def _(sp):
                sp.dma_start(x1_next, x1_d[0:P, :]).then_inc(x1_in, 16)
                sp.dma_start(sk_sb, sub_keys_t).then_inc(keys_in, 16)
                sp.dma_start(iota_sb[:, :], iota16).then_inc(iota_in, 16)
                sp.dma_start(final_gain[:, :], norm_final_g.partition_broadcast(P)).then_inc(final_gain_in, 16)
                with sp.Fori(1, TILES) as t:
                    sp.wait_ge(x1_copied, t)
                    sp.dma_start(x1_next, x1_d[rows(t), :]).then_inc(x1_in, 16)
                    sp.wait_ge(y_ready, t)
                    sp.dma_start(out[rows(t - 1), :], y).then_inc(y_out, 16)
                    sp.wait_ge(y_out, 16 * t)
                    sp.sem_inc(y_free, 1)
                sp.wait_ge(y_ready, TILES)
                sp.dma_start(out[S - P:S, :], y).then_inc(y_out, 16)
                sp.wait_ge(y_out, 16 * TILES)

            @block.gpsimd
            def _(pool):
                def step(t, g, s):
                    nc.gpsimd.tensor_copy(rowid[:, s, :], chosen[:, bass.ds(g * TOPK, TOPK)]).then_inc(ids_ready, 1)
                    pool.wait_ge(ids_ready, g + 1)
                    for table, ring_rows, arrived, used in ((peer_u, u_rows, u_in, u_used), (peer_v, v_rows, v_in, v_used)):
                        for j in range(TOPK):
                            slot = j % RING
                            pool.wait_ge(used, g * TOPK + j + 1)
                            settle(pool, passed)
                            pool.indirect_dma_start(ring_rows[:, slot, :], None, table[:, :],
                                                    bass.IndirectOffsetOnAxis(rowid[:, s, j:j + 1], 0)
                                                    ).then_inc(arrived[slot], 16)

                with pool.Fori(0, TILES) as t:
                    with pool.Fori(0, CHUNKS) as chunk:
                        pool.wait_ge(chosen_ready, t * CHUNKS + chunk + 1)
                        settle(pool, passed)
                        for s in range(CH):
                            step(t, (t * CHUNKS + chunk) * CH + s, s)

            def slot_value(g, j):
                return 16 * (g * (TOPK // RING) + j // RING + 1)

            @block.vector
            def _(dve):
                def top16(sets, values, to, to_index, done):
                    def stage(operation, signal=None):
                        for i in range(sets):
                            last = operation(i)
                        signal(last) if signal else topk.add(last)
                        if not signal:
                            topk.wait(dve)
                            settle(dve, passed)
                    settle(dve, passed)
                    stage(lambda i: nc.vector.max(to[:, i, 0:8], values[:, i, :]))
                    stage(lambda i: nc.vector.max_index(to_index[:, i, 0:8], to[:, i, 0:8], values[:, i, :]))
                    stage(lambda i: nc.vector.match_replace(values[:, i, :], to[:, i, 0:8], values[:, i, :], LOWEST))
                    stage(lambda i: nc.vector.max(to[:, i, 8:16], values[:, i, :]))
                    stage(lambda i: nc.vector.max_index(to_index[:, i, 8:16], to[:, i, 8:16], values[:, i, :]), done)

                def search(t, c):
                    topk.begin(t * CHUNKS + c)
                    ring.emptied(dve, t, 3 * c + SCORE)
                    top16(CS, scores, top, topi, lambda last: last.then_inc(scores_used, 1))

                def choose(t, c):
                    dve.wait_ge(scores_used, t * CHUNKS + c + 1)
                    pairs = top[:, :, :].rearrange("p (h i) k -> p h i k", i=2)
                    nc.vector.tensor_copy(topf[:, :, :], topi[:, :, :])
                    topk.add(nc.vector.tensor_tensor(
                        cand4, pairs[:, :, 0, :].unsqueeze(3).to_broadcast([P, CH, TOPK, TOPK]),
                        pairs[:, :, 1, :].unsqueeze(2).to_broadcast([P, CH, TOPK, TOPK]), ALU.add))
                    topk.wait(dve)
                    top16(CH, cand3, best, pos, topk.add)
                    topk.wait(dve)
                    per_head = shifted[:, :].rearrange("p (h k) -> p h k", h=CH)
                    nc.vector.tensor_tensor(per_head, best[:, :, :], best[:, :, 0:1].to_broadcast([P, CH, TOPK]),
                                            ALU.subtract).then_inc(shifted_ready, 1)
                    flat = pos[:, :, :].rearrange("p h k -> p (h k)")
                    nc.vector.tensor_scalar(half_pos[:, 0, :], flat, 4, None, ALU.logical_shift_right)
                    topk.add(nc.vector.tensor_scalar(half_pos[:, 1, :], flat, 15, None, ALU.bitwise_and))
                    topk.wait(dve)
                    topk.add(nc.vector.tensor_copy(half_f[:, :], half_pos[:, :, :].rearrange("p i n -> p (i n)")))
                    topk.wait(dve)
                    topk.add(nc.vector.tensor_tensor(
                        hit3, half_f[:, :].unsqueeze(2).to_broadcast([P, 2 * CK, TOPK]),
                        iota_sb[:, :].unsqueeze(1).to_broadcast([P, 2 * CK, TOPK]), ALU.is_equal))
                    topk.wait(dve)
                    keys = topf[:, :, :].rearrange("p (h i) k -> p h i k", i=2)
                    for i in range(2):
                        picked = nc.vector.tensor_tensor(
                            hit5[:, i, :, :, :], hit5[:, i, :, :, :],
                            keys[:, :, i, :].unsqueeze(2).to_broadcast([P, CH, TOPK, TOPK]), ALU.mult)
                    topk.add(picked)
                    topk.wait(dve)
                    topk.add(nc.vector.reduce_sum(found[:, :, :].rearrange("p i n -> p (i n)"), hit3, AX.X))
                    topk.wait(dve)
                    nc.vector.scalar_tensor_tensor(out=chosen[:, bass.ds((t * CHUNKS + c) * CK, CK)],
                                                   in0=found[:, 0, :], scalar=float(N_KEYS), in1=found[:, 1, :],
                                                   op0=ALU.mult, op1=ALU.add).then_inc(chosen_ready, 1)
                    assert topk.n == TOPK_STEPS, topk.n

                def normalise(t, c):
                    chunk = t * CHUNKS + c
                    normal.begin(chunk)
                    dve.wait_ge(wexp_ready, chunk + 1)
                    per_head = shifted[:, :].rearrange("p (h k) -> p h k", h=CH)
                    normal.add(nc.vector.reduce_sum(wsum[:, :], per_head, AX.X))
                    normal.wait(dve)
                    normal.add(nc.vector.reciprocal(rwsum[:, :], wsum[:, :]))
                    normal.wait(dve)
                    nc.vector.tensor_tensor(weight[:, :].rearrange("p (h k) -> p h k", h=CH), per_head,
                                            rwsum[:, :].unsqueeze(2).to_broadcast([P, CH, TOPK]), ALU.mult
                                            ).then_inc(weight_ready, 1)

                def norm(t):
                    dve.wait_ge(rms1_ready, t + 1)
                    nc.vector.reciprocal(small[:, 5:6], small[:, 4:5]).then_inc(rstd1_ready, 1)
                    dve.wait_ge(rstd1_ready, t + 1)
                    nc.vector.scalar_tensor_tensor(out=h2_next, in0=x1_next, scalar=small[:, 5:6], in1=gain[:, :],
                                                   op0=ALU.mult, op1=ALU.mult).then_inc(h2_ready, 1)

                def start(t):
                    dve.wait_ge(h2_ready, t + 1)
                    nc.vector.tensor_copy(h2_now, h2_next).then_inc(h2_copied, 1)
                    dve.wait_ge(h2_copied, t + 1)

                def step(t, hd, route):
                    g, s = t * PEER_HEADS + hd, hd % 2
                    for j in range(TOPK):
                        slot = j % RING
                        dve.wait_ge(u_in[slot], slot_value(g, j))
                        nc.vector.tensor_tensor_reduce(out=u_rows[:, slot, :], in0=u_rows[:, slot, :], in1=h2_now,
                                                       scale=1.0, scalar=0.0, op0=ALU.mult, op1=ALU.add,
                                                       accum_out=dots[:, s, j:j + 1]).then_inc(u_used, 1)
                    if s == 0:
                        normalise(t, hd // CH)
                        dve.wait_ge(weight_ready, t * CHUNKS + hd // CH + 1)
                    dve.wait_ge(gelu_ready, g + 1)
                    nc.vector.tensor_tensor(coef[:, s, :], gelu[:, s, :], weight[:, s * TOPK:(s + 1) * TOPK], ALU.mult
                                            ).then_inc(coef_ready, 1)
                    route()

                def end(t):
                    dve.wait_ge(v_used, RING + HK * (t + 1))
                    dve.wait_ge(x1_copied, t + 1)
                    dve.wait_ge(rstd_ready, t + 1)
                    for c in range(2):
                        part = slice(c * BANK, (c + 1) * BANK)
                        nc.vector.tensor_tensor(x2[:, part], acc[c][:, :], x1_now[:, part], ALU.add).then_inc(x2_ready, 1)
                    dve.wait_ge(rms_ready, t + 1)
                    nc.vector.reciprocal(small[:, 2:3], small[:, 1:2]).then_inc(rstd_ready, 1)
                    dve.wait_ge(rstd_ready, t + 2)
                    dve.wait_ge(final_gain_in, 16)
                    nc.vector.scalar_tensor_tensor(out=y, in0=x2, scalar=small[:, 2:3], in1=final_gain[:, :],
                                                   op0=ALU.mult, op1=ALU.mult).then_inc(y_ready, 1)

                dve.sem_inc(u_used, RING)
                dve.sem_inc(x2_ready, 2)
                dve.sem_inc(rstd_ready, 1)
                dve.sem_inc(y_free, 1)
                dve.wait_ge(iota_in, 16)
                dve.wait_ge(gain2_in, 16)
                experts_with_route(dve, start, step, end, nothing, norm, search, choose)

            @block.scalar
            def _(act):
                def measure(t):
                    act.wait_ge(x1_in, 16 * t + 16)
                    nc.scalar.activation(h2_next, x1_next, ACT.Square, accum_out=small[:, 3:4]).then_inc(sumsq1_ready, 1)
                    act.wait_ge(sumsq1_ready, t + 1)
                    nc.scalar.activation(small[:, 4:5], small[:, 3:4], ACT.Sqrt, bias=small[:, 14:15],
                                         scale=1.0 / D).then_inc(rms1_ready, 1)

                def start(t):
                    act.wait_ge(x2_ready, 2 * t + 2)
                    act.wait_ge(h2_ready, t + 1)
                    nc.scalar.activation(x1_now, x1_next, ACT.Copy).then_inc(x1_copied, 1)

                def search(t, c):
                    if c == 0:
                        for half in range(2):
                            bank = turned.filled(act, t, half)
                            nc.scalar.activation(h2T[:, half * BANK:(half + 1) * BANK], bank[:, :], ACT.Copy
                                                 ).then_inc(turned.free, 1)
                    for use, to in ((QUERY, q_sb), (QUERYT, qT.rearrange("p s n -> p (s n)")),
                                    (SCORE, scores[:, :, :].rearrange("p s n -> p (s n)"))):
                        bank = ring.filled(act, t, 3 * c + use)
                        if use == SCORE:
                            after(act, scores_used, CHUNKS * t + c)
                        nc.scalar.activation(to, bank[:, :], ACT.Copy).then_inc(ring.free, 1)

                def choose(t, c):
                    act.wait_ge(shifted_ready, t * CHUNKS + c + 1)
                    nc.scalar.activation(shifted[:, :], shifted[:, :], ACT.Exp).then_inc(wexp_ready, 1)

                def step(t, hd, route):
                    g, s = t * PEER_HEADS + hd, hd % 2
                    if s == 0:
                        route()
                    act.wait_ge(u_used, RING + TOPK * (g + 1))
                    nc.scalar.activation(gelu[:, s, :], dots[:, s, :], ACT.Gelu).then_inc(gelu_ready, 1)
                    act.wait_ge(coef_ready, g + 1)
                    for j in range(TOPK):
                        act.wait_ge(v_used, g * TOPK + j + 1 + RING - DIAGS)
                        nc.scalar.activation(diag[:, j % DIAGS, :], ident[:, :], ACT.Copy, scale=coef[:, s, j:j + 1]
                                             ).then_inc(diag_ready, 1)
                    if s == 1:
                        route()

                def end(t):
                    act.wait_ge(x2_ready, 2 * t + 4)
                    act.wait_ge(y_free, t + 1)
                    nc.scalar.activation(y, x2, ACT.Square, accum_out=small[:, 0:1]).then_inc(sumsq_ready, 1)
                    act.wait_ge(sumsq_ready, t + 1)
                    nc.scalar.activation(small[:, 1:2], small[:, 0:1], ACT.Sqrt, bias=small[:, 14:15],
                                         scale=1.0 / D).then_inc(rms_ready, 1)

                ring.open(act)
                turned.open(act)
                experts_with_route(act, start, step, end, measure, nothing, search, choose)

            @block.tensor
            def _(pe):
                def search(t, c):
                    if c == 0:
                        pe.wait_ge(h2_ready, t + 1)
                        for half in range(2):
                            bank = turned.claim(pe, t, half)
                            for k in range(KC // 2):
                                at = half * BANK + k * P
                                last = nc.tensor.transpose(bank[:, k * P:(k + 1) * P], h2_next[:, at:at + P], ident[:, :])
                            last.then_inc(turned.full, 1)
                        turned.emptied(pe, t, 1)
                    bank = ring.claim(pe, t, 3 * c + QUERY)
                    for k in range(KC):
                        last = nc.tensor.matmul(bank[:, :], h2T[:, k * P:(k + 1) * P],
                                                wq_sb[:, k, c * BANK:(c + 1) * BANK],
                                                start=(k == 0), stop=(k == KC - 1))
                    last.then_inc(ring.full, 1)
                    ring.emptied(pe, t, 3 * c + QUERY)
                    bank = ring.claim(pe, t, 3 * c + QUERYT)
                    for i in range(CS):
                        last = nc.tensor.transpose(bank[:, i * P:(i + 1) * P], q_sb[:, i * P:(i + 1) * P], ident[:, :])
                    last.then_inc(ring.full, 1)
                    ring.emptied(pe, t, 3 * c + QUERYT)
                    if isinstance(t, int) and t + c == 0:
                        pe.wait_ge(keys_in, 16)
                    bank = ring.claim(pe, t, 3 * c + SCORE)
                    for i in range(CS):
                        last = nc.tensor.matmul(bank[:, i * P:(i + 1) * P], qT[:, i, :], sk_sb[:, c * CS + i, :],
                                                start=True, stop=True)
                    last.then_inc(ring.full, 1)

                def start(t):
                    pe.wait_ge(x2_ready, 2 * t + 2)

                def step(t, hd, route):
                    g = t * PEER_HEADS + hd
                    route()
                    for j in range(TOPK):
                        slot = j % RING
                        pe.wait_ge(diag_ready, g * TOPK + j + 1)
                        pe.wait_ge(v_in[slot], slot_value(g, j))
                        for c in range(2):
                            last = nc.tensor.matmul(acc[c][:, :], diag[:, j % DIAGS, :],
                                                    v_rows[:, slot, c * BANK:(c + 1) * BANK],
                                                    start=(hd == 0 and j == 0), stop=True, skip_group_check=True)
                        last.then_inc(v_used, 1)

                pe.sem_inc(v_used, RING)
                pe.wait_ge(wq_in, 16)
                experts_with_route(pe, start, step, nothing, nothing, nothing, search, nothing)


_INS = ["x", "norm1_g", "w_in", "sink_logits", "pool_w", "pool_scale", "w_branch", "w_gate", "b_gate", "w_out",
        "norm2_g", "peer_w_query", "peer_sub_keys", "peer_u", "peer_v", "norm_final_g"]


def _constants(S):
    import numpy as np
    q, c = np.arange(P)[:, None], np.arange(3 * P)[None, :]
    dist = np.abs(q + P - c).astype(np.float32)
    slopes = np.array([2.0 ** (-8.0 * (h + 1) / QH) for h in range(QH)], np.float32)
    tiles = S // P
    windows = (2, 4, 8, 16)
    table = np.zeros((tiles, P, QH * 3 * P + GROUPS), np.float32)
    for t in range(tiles):
        s_abs = (t - 1) * P + c
        valid = (dist <= P) & (s_abs >= 0) & (s_abs < S)
        bias = np.where(valid[None], -slopes[:, None, None] * dist[None], np.float32(-1e30))
        table[t, :, :QH * 3 * P] = bias.transpose(1, 0, 2).reshape(P, -1)
        for g, w in enumerate(windows):
            at = t * P + np.arange(P)
            n = np.clip(at + w - w // 2, 0, S) - np.clip(at - w // 2, 0, S)
            table[t, :, QH * 3 * P + g] = np.float32(1.0) / n.astype(np.float32)
    band = np.zeros((P, 3, GROUPS, P), np.float32)
    s, t = np.arange(P)[:, None], np.arange(P)[None, :]
    for b in range(3):
        for g, w in enumerate(windows):
            d = s + (b - 1) * P - t
            band[:, b, g, :] = (d >= -(w // 2)) & (d < w - w // 2)
    return {"identity": np.eye(P, dtype=np.float32), "band": band,
            "bias_table": table.reshape(tiles * P, -1),
            "iota16": np.tile(np.arange(TOPK, dtype=np.float32), (P, 1))}


def kernel(**inputs):
    import numpy as np
    import concourse.bacc as bacc
    from concourse.bass_utils import run_bass_kernel_spmd

    a = {n: np.asarray(inputs[n]) for n in _INS}
    S, D = a["x"].shape[1:]
    lay = {
        "x": a["x"][0], "norm1_g": a["norm1_g"][0], "w_in": a["w_in"][0], "sink_logits": a["sink_logits"][0],
        "pool_w": a["pool_w"][0], "pool_scale": a["pool_scale"][0].reshape(GROUPS, P).T,
        "w_branch": a["w_branch"][0].reshape(-1, D), "w_gate": a["w_gate"][0], "b_gate": a["b_gate"][0],
        "w_out": a["w_out"][0], "norm2_g": a["norm2_g"][0], "w_query": a["peer_w_query"][0],
        "sub_keys_t": a["peer_sub_keys"][0].transpose(3, 0, 1, 2).reshape(P, PEER_HEADS * 2, N_KEYS),
        "peer_u": a["peer_u"][0], "peer_v": a["peer_v"][0], "norm_final_g": a["norm_final_g"],
    }
    lay.update(_constants(S))
    nc = bacc.Bacc("TRN2", target_bir_lowering=False, num_devices=1)
    arrays, args = {}, {}
    for name, value in lay.items():
        arrays[f"in_{name}"] = np.ascontiguousarray(value)
        args[name] = nc.dram_tensor(f"in_{name}", value.shape, mybir.dt.from_np(value.dtype), kind="ExternalInput").ap()
    out = nc.dram_tensor("out_0", (S, D), F32, kind="ExternalOutput").ap()
    encoder_block(nc, out=out, **args)
    r = run_bass_kernel_spmd(nc, [arrays], core_ids=[0])
    return r.results[0]["out_0"].reshape(1, S, D)
```
